# Optimizing a Trainium2 kernel written in Bass

```python
import jax, jax.numpy as jnp
from jax import lax
import numpy as np

D_MODEL = 1024
BATCH = 1
SEQ = 512
DEPTH = 2

N_MIXERS = 2
N_A_LAYERS = (DEPTH + 1) // 2
N_B_LAYERS = DEPTH // 2
D_FF = 2816
CHUNK = 128
A_INNER = D_MODEL
A_GROUPS = 8
A_GROUP_DIM = A_INNER // A_GROUPS
B_HEADS = 16
B_HEAD_DIM = D_MODEL // B_HEADS
Q_BLOCK = 128
RMS_EPS = 1e-6
LN_EPS = 1e-5

kernel_name = "hybrid_gmlp_stickbreak_macaron"

def rms_norm(x, g):
    xf = x.astype(jnp.float32)
    y = xf * lax.rsqrt(jnp.mean(xf * xf, axis=-1, keepdims=True) + RMS_EPS)
    return (y * g.astype(jnp.float32)).astype(x.dtype)

def layer_norm(x, g):
    xf = x.astype(jnp.float32)
    mu = jnp.mean(xf, axis=-1, keepdims=True)
    var = jnp.mean(jnp.square(xf - mu), axis=-1, keepdims=True)
    return ((xf - mu) * lax.rsqrt(var + LN_EPS) * g.astype(jnp.float32)).astype(x.dtype)

def swiglu(x, w_gate, w_up, w_down):
    return (jax.nn.silu(x @ w_gate) * (x @ w_up)) @ w_down

def chunked_gmlp(x, w_in, ln_g, w_s, b_s, w_out):
    bsz, seq, _ = x.shape
    h = jax.nn.gelu(x @ w_in, approximate=False)
    u, v = jnp.split(h, 2, axis=-1)
    v = layer_norm(v, ln_g)
    v = v.reshape(bsz, seq // CHUNK, CHUNK, A_GROUPS, A_GROUP_DIM)
    causal = jnp.tril(jnp.ones((CHUNK, CHUNK), dtype=bool))
    w = jnp.where(causal[None], w_s, 0.0).astype(v.dtype)
    bias = jnp.swapaxes(b_s, 0, 1)[None, None, :, :, None].astype(v.dtype)
    v = jnp.einsum('gts,bcsgd->bctgd', w, v) + bias
    y = u * v.reshape(bsz, seq, A_INNER)
    return y @ w_out

def stick_breaking_attention(x, w_qkv, w_o):
    bsz, seq, _ = x.shape
    qkv = (x @ w_qkv).reshape(bsz, seq, 3, B_HEADS, B_HEAD_DIM)
    q = jnp.moveaxis(qkv[:, :, 0], 1, 2)
    k = jnp.moveaxis(qkv[:, :, 1], 1, 2)
    v = jnp.moveaxis(qkv[:, :, 2], 1, 2)
    scale = B_HEAD_DIM ** -0.5
    outs = []
    for blk in range(seq // Q_BLOCK):
        q0 = blk * Q_BLOCK
        kend = q0 + Q_BLOCK
        qb = q[:, :, q0:kend].astype(jnp.float32)
        kb = k[:, :, :kend].astype(jnp.float32)
        vb = v[:, :, :kend]
        z = jnp.einsum('bhqd,bhkd->bhqk', qb, kb) * scale
        t_idx = q0 + jnp.arange(Q_BLOCK)[:, None]
        s_idx = jnp.arange(kend)[None, :]
        strict = s_idx < t_idx
        log_keep = jnp.where(strict, jax.nn.log_sigmoid(-z), 0.0)
        later = lax.cumsum(log_keep, axis=3, reverse=True) - log_keep
        log_a = jax.nn.log_sigmoid(z) + later
        a = jnp.where(strict, jnp.exp(log_a), 0.0)
        outs.append(jnp.einsum('bhqk,bhkd->bhqd', a.astype(vb.dtype), vb))
    o = jnp.concatenate(outs, axis=2)
    o = jnp.moveaxis(o, 1, 2).reshape(bsz, seq, B_HEADS * B_HEAD_DIM)
    return o @ w_o

def setup_inputs(seed: int = 0) -> dict:
    key = jax.random.key(seed)
    ks = jax.random.split(key, 16)
    f32 = jnp.float32

    def dense(k, shape, fan_in):
        return jax.random.normal(k, shape, f32) * (fan_in ** -0.5)

    x = jax.random.normal(ks[0], (BATCH, SEQ, D_MODEL), f32)
    norm_pre = 1.0 + 0.05 * jax.random.normal(ks[1], (DEPTH, 3, D_MODEL), f32)
    norm_post = 1.0 + 0.05 * jax.random.normal(ks[2], (DEPTH, 3, D_MODEL), f32)
    ffn_w_gate = dense(ks[3], (DEPTH, 2, D_MODEL, D_FF), D_MODEL)
    ffn_w_up = dense(ks[4], (DEPTH, 2, D_MODEL, D_FF), D_MODEL)
    ffn_w_down = dense(ks[5], (DEPTH, 2, D_FF, D_MODEL), D_FF)
    a_w_in = dense(ks[6], (N_A_LAYERS, D_MODEL, 2 * A_INNER), D_MODEL)
    a_ln_g = 1.0 + 0.05 * jax.random.normal(ks[7], (N_A_LAYERS, A_INNER), f32)
    a_w_s = dense(ks[8], (N_A_LAYERS, A_GROUPS, CHUNK, CHUNK), CHUNK)
    a_b_s = 1.0 + 0.1 * jax.random.normal(ks[9], (N_A_LAYERS, A_GROUPS, CHUNK), f32)
    a_w_out = dense(ks[10], (N_A_LAYERS, A_INNER, D_MODEL), A_INNER)
    b_w_qkv = dense(ks[11], (N_B_LAYERS, D_MODEL, 3 * D_MODEL), D_MODEL)
    b_w_o = dense(ks[12], (N_B_LAYERS, D_MODEL, D_MODEL), D_MODEL)
    return {"x": x, "norm_pre": norm_pre, "norm_post": norm_post,
            "ffn_w_gate": ffn_w_gate, "ffn_w_up": ffn_w_up, "ffn_w_down": ffn_w_down,
            "a_w_in": a_w_in, "a_ln_g": a_ln_g, "a_w_s": a_w_s, "a_b_s": a_b_s,
            "a_w_out": a_w_out, "b_w_qkv": b_w_qkv, "b_w_o": b_w_o}

def reference(x, norm_pre, norm_post, ffn_w_gate, ffn_w_up, ffn_w_down,
              a_w_in, a_ln_g, a_w_s, a_b_s, a_w_out, b_w_qkv, b_w_o):
    h = x
    for layer in range(DEPTH):
        f = swiglu(rms_norm(h, norm_pre[layer, 0]),
                   ffn_w_gate[layer, 0], ffn_w_up[layer, 0], ffn_w_down[layer, 0])
        h = h + 0.5 * rms_norm(f, norm_post[layer, 0])
        hn = rms_norm(h, norm_pre[layer, 1])
        if layer % N_MIXERS == 0:
            ia = layer // N_MIXERS
            m = chunked_gmlp(hn, a_w_in[ia], a_ln_g[ia], a_w_s[ia], a_b_s[ia], a_w_out[ia])
        else:
            ib = layer // N_MIXERS
            m = stick_breaking_attention(hn, b_w_qkv[ib], b_w_o[ib])
        h = h + rms_norm(m, norm_post[layer, 1])
        f = swiglu(rms_norm(h, norm_pre[layer, 2]),
                   ffn_w_gate[layer, 1], ffn_w_up[layer, 1], ffn_w_down[layer, 1])
        h = h + 0.5 * rms_norm(f, norm_post[layer, 2])
    return h


_drawn_inputs = setup_inputs


def setup_inputs(seed=0):
    import zlib

    import numpy as np

    out = dict(_drawn_inputs(seed))
    spreads = {}
    factors = {}
    for name, (base, spread) in spreads.items():
        noise = np.random.default_rng([zlib.crc32(name.encode()), seed]).standard_normal(out[name].shape)
        drawn = base * np.exp(spread * noise) if base else spread * noise
        out[name] = __import__('jax').numpy.asarray(drawn.astype(out[name].dtype))
    for name, factor in factors.items():
        out[name] = (out[name] * factor).astype(out[name].dtype)
    return out
```

```python
from contextlib import ExitStack

import concourse.bass as bass
from concourse import mybir
from concourse.alu_op_type import AluOpType as ALU

ACT = mybir.ActivationFunctionType
F32 = mybir.dt.float32
F32R = mybir.dt.float32r
BF16 = mybir.dt.bfloat16

P = 128
DM = 1024
KC = DM // P
T = 512
TT = T // P
DFF = 2816
NF = DFF // P
UNIT = 1024
G = 8
RMS_EPS = 1e-6
LN_EPS = 1e-5
HD = 64
HEAD_PAIRS = 8
QSCALE = HD ** -0.5
MASKED = -1e30

BQ = [0, 128, 256, 256]
BOFF = [0, 512, 896, 1152]
BPOS = [(0, 0), (1, 128), (2, 0), (2, 256)]
AW = 1408
PIECES = [(0, 512, 0, 512), (640, 1536, 512, 1408)]

SUBS = [("ffn", 0, 0), ("gmlp", 0, 0), ("ffn", 0, 1), ("ffn", 1, 0), ("attn", 0, 0), ("ffn", 1, 1)]
PAIRS = {"ffn": NF + NF // 2, "gmlp": 12, "attn": 16}
BASE = [sum(PAIRS[k] for k, _, _ in SUBS[:s]) for s in range(len(SUBS) + 1)]
NPAIR = BASE[-1]
NSUB = len(SUBS)
EARLY = 4
OWN_ADDS = 2


def slots(pair):
    return 2 * (pair % 2), 2 * (pair % 2) + 1


def build(nc, x, norm_pre, norm_post, w_gate, w_up, w_down, a_w_in, a_ln_g, a_w_s, a_b_s, a_w_out,
          b_w_qkv, b_w_o, out):
    ctx = ExitStack()
    with ctx:
        cursor = [(nc.sbuf_base + 31) // 32 * 32]

        def place(name, shape, dt=F32, at=None):
            n = (4 if dt != BF16 else 2)
            for d in shape[1:]:
                n *= d
            if at is None:
                at = cursor[0]
                cursor[0] += (n + 31) // 32 * 32
            return nc.alloc_sbuf_tensor_at(name, shape, dt, offset=at), at + n

        def sb(name, shape, dt=F32):
            return place(name, shape, dt)[0]

        h = sb("h", [P, KC, T])
        xn_at = cursor[0]
        xn_hi = sb("xn_hi", [P, KC, T], F32R)
        xn_lo = sb("xn_lo", [P, KC, T], F32R)
        raw = sb("raw", [P, 2, UNIT])
        w_hi = sb("w_hi", [P, 4, UNIT], F32R)
        w_lo = sb("w_lo", [P, 4, UNIT], F32R)
        sqa_at = cursor[0]
        sqa = sb("sqa", [P, T])
        sqb_at = cursor[0]
        sqb = sb("sqb", [P, T])
        diag = sb("diag", [P, TT, P])
        rbc = sb("rbc", [P, T])
        ident = sb("ident", [P, P])
        ones = sb("ones", [P, P])
        neg_tri = sb("neg_tri", [P, P], F32R)
        neg_ones = sb("neg_ones", [P, P], F32R)
        ident_bf = sb("ident_bf", [P, P], BF16)
        mask_bf = sb("mask_bf", [P, 2 * P], BF16)
        NG = 12 * KC + KC
        gcol = sb("gcol", [P, NG])
        std = sb("std", [P, 2, TT])
        rstd = sb("rstd", [P, 2, TT])
        s_tok = sb("s_tok", [P, TT])
        e2 = sb("e2", [P, TT])
        eps_col = sb("eps_col", [P, 2])

        region = cursor[0]
        m, after_m = place("m", [P, KC, T], at=region)
        sq, after_sq = place("sq", [P, KC, T], at=after_m)
        t1, a1 = place("t1", [P, 2, T], at=region)
        yf, _ = place("yf", [P, 2, T], at=a1)
        hid_hi, a1 = place("hid_hi", [P, NF, T], F32R, at=after_m)
        hid_lo, end_ffn = place("hid_lo", [P, NF, T], F32R, at=a1)
        u, a1 = place("u", [P, KC, T], at=after_m)
        v, a1 = place("v", [P, TT, DM], at=a1)
        y_hi, a1 = place("y_hi", [P, KC, T], F32R, at=a1)
        y_lo, a1 = place("y_lo", [P, KC, T], F32R, at=a1)
        wsT, a1 = place("wsT", [P, G, P], at=a1)
        bias_bc, a1 = place("bias_bc", [P, G, P], at=a1)
        vst, a1 = place("vst", [P, 40], at=a1)
        ws_raw, _ = place("ws_raw", [P, G, P], at=region)
        ut, a1 = place("ut", [P, 2, T], at=region + 4096)
        yt, a1 = place("yt", [P, 2, T], at=a1)
        vsq, _ = place("vsq", [P, DM], at=a1)
        e_t, a1 = place("e_t", [P, 2, AW], at=region)
        p_hi, a1 = place("p_hi", [P, 2, AW], F32R, at=a1)
        p_lo, a1 = place("p_lo", [P, 2, AW], F32R, at=a1)
        assert a1 >= after_sq
        o_hi, a1 = place("o_hi", [P, KC, T], F32R, at=a1)
        o_lo, a1 = place("o_lo", [P, KC, T], F32R, at=a1)
        vt, a1 = place("vt", [P, TT, DM], at=a1)
        qk_hi, a1 = place("qk_hi", [P, 2, 2, T], F32R, at=a1)
        qk_lo, a1 = place("qk_lo", [P, 2, 2, T], F32R, at=a1)
        qy, end_attn = place("qy", [P, 2, T], at=a1)
        vp_hi, _ = place("vp_hi", [P, TT, P], F32R, at=sqa_at)
        vp_lo, _ = place("vp_lo", [P, TT, P], F32R, at=sqb_at)
        part, _ = place("part", [P, EARLY, T], at=xn_at)
        x_in, _ = place("x_in", [P, TT, DM], at=after_m)
        g_rows, _ = place("g_rows", [P, P], at=after_m + 16384)
        tri_f, _ = place("tri_f", [P, 4, P], at=after_m + 20480)
        o_tok, _ = place("o_tok", [P, TT, DM], at=after_m)
        assert max(end_ffn, end_attn) <= nc.sbuf_usable_end, (end_ffn, end_attn, nc.sbuf_usable_end)

        psum = ctx.enter_context(nc.psum_tensor("psum", [P, 8 * T], F32))
        bank = [psum[:, i * T:(i + 1) * T] for i in range(8)]

        def sem(name):
            return ctx.enter_context(nc.semaphore(name))

        x_loaded = sem("x_loaded")
        g_loaded = sem("g_loaded")
        gm_loaded = sem("gm_loaded")
        const_ready = sem("const_ready")
        const2_ready = sem("const2_ready")
        turned = sem("turned")
        gains_ready = sem("gains_ready")
        raw_loaded = [sem("raw_loaded0"), sem("raw_loaded1")]
        hi_ready = sem("hi_ready")
        lo_ready = sem("lo_ready")
        w_used = sem("w_used")
        acc_done = sem("acc_done")
        m_evac = sem("m_evac")
        msq_ready = sem("msq_ready")
        msum_done = sem("msum_done")
        ss_ready = sem("ss_ready")
        s_ready = sem("s_ready")
        std_ready = sem("std_ready")
        rstd_ready = sem("rstd_ready")
        diag_ready = sem("diag_ready")
        bc_ready = sem("bc_ready")
        rbc_ready = sem("rbc_ready")
        e2_ready = sem("e2_ready")
        applied = sem("applied")
        h_ready = sem("h_ready")
        xhi_ready = sem("xhi_ready")
        xlo_ready = sem("xlo_ready")
        hsq_ready = sem("hsq_ready")
        hsum_even = sem("hsum_even")
        hsum_odd = sem("hsum_odd")
        t1_ready = sem("t1_ready")
        silu_ready = sem("silu_ready")
        y_ready = sem("y_ready")
        hid_hi_ready = sem("hid_hi_ready")
        hid_lo_ready = sem("hid_lo_ready")
        v_ready = sem("v_ready")
        ln_step = sem("ln_step")
        ln_sq = sem("ln_sq")
        ln_std = sem("ln_std")
        vn_ready = sem("vn_ready")
        ws_masked = sem("ws_masked")
        ws_turned = sem("ws_turned")
        ws_ready = sem("ws_ready")
        ut_ready = sem("ut_ready")
        u_ready = sem("u_ready")
        sp_done = sem("sp_done")
        yt_ready = sem("yt_ready")
        ym_ready = sem("ym_ready")
        yhi_ready = sem("yhi_ready")
        ylo_ready = sem("ylo_ready")
        vp_copied = sem("vp_copied")
        vp_ready = sem("vp_ready")
        qy_ready = sem("qy_ready")
        qk_hi_ready = sem("qk_hi_ready")
        qk_lo_ready = sem("qk_lo_ready")
        z_ready = sem("z_ready")
        e_step = sem("e_step")
        part_done = sem("part_done")
        part_ready = sem("part_ready")
        sp_ready = sem("sp_ready")
        sphi_ready = sem("sphi_ready")
        splo_ready = sem("splo_ready")
        loga_ready = sem("loga_ready")
        a_ready = sem("a_ready")
        ahi_ready = sem("ahi_ready")
        alo_ready = sem("alo_ready")
        o_ready = sem("o_ready")
        ohi_ready = sem("ohi_ready")
        olo_ready = sem("olo_ready")
        out_turned = sem("out_turned")
        out_even = sem("out_even")
        out_odd = sem("out_odd")
        stored = sem("stored")

        def gain(pre, s, d):
            _, layer, j = SUBS[s]
            j = {"ffn": 2 * j, "gmlp": 1, "attn": 1}[SUBS[s][0]]
            at = (0 if pre else 6 * KC) + (layer if SUBS[s][0] != "attn" else 1) * 3 * KC + j * KC + d
            return gcol[:, at:at + 1]

        def acc_base(s):
            return (KC - 1) * sum(k != "attn" for k, _, _ in SUBS[:s])

        def ffn_index(s):
            return sum(k == "ffn" for k, _, _ in SUBS[:s])

        Z0 = [0, 3 * T]

        block = ctx.enter_context(nc.Block())

        @block.sync
        def _(sp):
            for tt in range(TT):
                sp.dma_start(x_in[:, tt, :], x[0, tt * P:(tt + 1) * P, :]).then_inc(x_loaded, 16)
            sp.dma_start(g_rows[0:48, :], norm_pre.rearrange("l j (c p) -> (l j c) p", p=P)).then_inc(g_loaded, 16)
            sp.dma_start(g_rows[48:96, :], norm_post.rearrange("l j (c p) -> (l j c) p", p=P)).then_inc(g_loaded, 16)
            sp.dma_start(g_rows[96:104, :], a_ln_g.rearrange("l (c p) -> (l c) p", p=P)).then_inc(g_loaded, 16)

            def load(n, par, src, view):
                if not (isinstance(n, int) and n < 2):
                    sp.wait_ge(lo_ready, n - 1)
                sp.dma_start(view(raw[:, par, :]), src).then_inc(raw_loaded[par], 16)

            def by_k(dst):
                return dst.rearrange("p (k f) -> p k f", k=KC)

            def by_half(dst):
                return dst.rearrange("p (k f) -> p k f", k=2)

            def flat(dst):
                return dst

            for s, (kind, layer, j) in enumerate(SUBS):
                n0 = 2 * BASE[s]
                if kind == "ffn":
                    gate = w_gate[layer, j].rearrange("(k p) f -> p k f", p=P)
                    up = w_up[layer, j].rearrange("(k p) f -> p k f", p=P)
                    first = 1 if s == 0 else 0
                    for f in range(first):
                        load(n0 + 2 * f, 0, gate[:, :, f * P:(f + 1) * P], by_k)
                        load(n0 + 2 * f + 1, 1, up[:, :, f * P:(f + 1) * P], by_k)
                    with sp.Fori(first, NF) as f:
                        load(n0 + 2 * f, 0, gate[:, :, bass.ds(f * P, P)], by_k)
                        load(n0 + 2 * f + 1, 1, up[:, :, bass.ds(f * P, P)], by_k)
                    n1 = n0 + 2 * NF
                    with sp.Fori(0, NF // 2) as i:
                        for c in range(2):
                            load(n1 + 2 * i + c, c, w_down[layer, j, bass.ds((2 * i + c) * P, P), :], flat)
                    continue
                w = (a_w_in if kind == "gmlp" else b_w_qkv)[0].rearrange("(k p) n -> p k n", p=P)
                v0 = DM if kind == "gmlp" else 2 * DM
                n = n0

                def load_v(n, c):
                    for q in range(4):
                        load(n + q, q % 2, w[:, 2 * q:2 * q + 2, v0 + c * T:v0 + (c + 1) * T], by_half)

                load_v(n0, 0)
                if kind == "gmlp":
                    for e in range(2):
                        load(n0 + 4 + e, e, w[:, :, e * P:(e + 1) * P], by_k)
                    load_v(n0 + 6, 1)
                    sp.wait_ge(hi_ready, n0 + 6)
                    sp.wait_ge(w_used, n0 + 2)
                    sp.wait_ge(rbc_ready, s + 1)
                    sp.dma_start(ws_raw[:, :, :], a_w_s[0].rearrange("g t s -> t g s")).then_inc(gm_loaded, 16)
                    sp.dma_start(bias_bc[:, :, :].rearrange("p g t -> p (g t)"),
                                 a_b_s[0].rearrange("g t -> (g t)").partition_broadcast(P)).then_inc(gm_loaded, 16)
                    for e in range(2, 8):
                        load(n0 + 8 + e, e % 2, w[:, :, e * P:(e + 1) * P], by_k)
                    n1 = n0 + 16
                else:
                    load(n0 + 4, 0, w[:, :, 0:P], by_k)
                    load(n0 + 5, 1, w[:, :, DM:DM + P], by_k)
                    load_v(n0 + 6, 1)
                    with sp.Fori(1, HEAD_PAIRS) as p:
                        load(n0 + 8 + 2 * p, 0, w[:, :, bass.ds(p * P, P)], by_k)
                        load(n0 + 9 + 2 * p, 1, w[:, :, bass.ds(p * P + DM, P)], by_k)
                    w_o = b_w_o[0].rearrange("(k p) n -> p k n", p=P)
                    with sp.Fori(0, KC // 2) as i:
                        for c in range(2):
                            load(n0 + 24 + 2 * i + c, c, w_o[:, :, bass.ds((2 * i + c) * P, P)], by_k)
                    continue
                with sp.Fori(0, KC // 2) as i:
                    for c in range(2):
                        load(n1 + 2 * i + c, c, a_w_out[0, bass.ds((2 * i + c) * P, P), :], flat)
            for tt in range(TT):
                sp.wait_ge(out_even, tt + 1)
                sp.wait_ge(out_odd, tt + 1)
                sp.dma_start(out[0, tt * P:(tt + 1) * P, :], o_tok[:, tt, :]).then_inc(stored, 16)
            sp.wait_ge(stored, 16 * TT)

        @block.gpsimd
        def _(pool):
            pool.memset(ident[:, :], 0.0).then_inc(const_ready, 1)
            pool.memset(ones[:, :], 1.0).then_inc(const_ready, 1)
            pool.memset(eps_col[:, 0:1], RMS_EPS).then_inc(const_ready, 1)
            pool.memset(eps_col[:, 1:2], LN_EPS).then_inc(const_ready, 1)
            pool.memset(tri_f[:, 0, :], -1.0).then_inc(const_ready, 1)
            pool.memset(tri_f[:, 1, :], -1.0).then_inc(const_ready, 1)
            pool.memset(tri_f[:, 2:4, :], MASKED).then_inc(const_ready, 1)
            pool.wait_ge(const_ready, 7)
            pool.affine_select(out=ident[:, :], in_=ident[:, :], compare_op=ALU.not_equal, fill=1.0,
                               base=0, pattern=[[-1, P]], channel_multiplier=1).then_inc(const_ready, 1)
            pool.affine_select(out=tri_f[:, 0, :], in_=tri_f[:, 0, :], compare_op=ALU.is_ge, fill=0.0,
                               base=0, pattern=[[-1, P]], channel_multiplier=1).then_inc(const_ready, 1)
            pool.affine_select(out=tri_f[:, 3, :], in_=tri_f[:, 3, :], compare_op=ALU.is_ge, fill=0.0,
                               base=0, pattern=[[-1, P]], channel_multiplier=1).then_inc(const_ready, 1)

            def pre_sums(s):
                pool.wait_ge(hsq_ready, 8 * s + 3)
                pool.tensor_tensor(sqa[:, :], m[:, 0, :], m[:, 2, :], ALU.add).then_inc(hsum_even, 1)
                for i, d in enumerate((4, 6)):
                    pool.wait_ge(hsq_ready, 8 * s + d + 1)
                    pool.wait_ge(hsum_even, 3 * s + i + 1)
                    pool.tensor_tensor(sqa[:, :], sqa[:, :], m[:, d, :], ALU.add).then_inc(hsum_even, 1)

            def post(s):
                for i, d in enumerate(range(1, 5)):
                    pool.wait_ge(msq_ready, 8 * s + d + 1)
                    if d == 1:
                        pool.tensor_tensor(sqa[:, :], sq[:, 0, :], sq[:, 1, :], ALU.add).then_inc(msum_done, 1)
                    else:
                        pool.wait_ge(msum_done, 4 * s + i)
                        pool.tensor_tensor(sqa[:, :], sqa[:, :], sq[:, d, :], ALU.add).then_inc(msum_done, 1)
                for d in range(OWN_ADDS, KC):
                    pool.wait_ge(applied, 8 * s + d + 1)
                    pool.tensor_tensor(h[:, d, :], h[:, d, :], m[:, d, :], ALU.add).then_inc(h_ready, 1)

            for s, (kind, _, _) in enumerate(SUBS):
                pre_sums(s)
                if kind == "gmlp":
                    pool.wait_ge(gm_loaded, 32)
                    pool.affine_select(out=ws_raw[:, :, :], in_=ws_raw[:, :, :], compare_op=ALU.is_ge, fill=0.0,
                                       base=0, pattern=[[0, G], [-1, P]], channel_multiplier=1).then_inc(ws_masked, 1)
                if kind == "attn":
                    b = BASE[s]

                    def split_unit(pair, par, c):
                        pool.wait_ge(hi_ready, 2 * pair + c + 1)
                        pool.wait_ge(lo_ready, 2 * pair + c)
                        pool.tensor_tensor(w_lo[:, 2 * par + c, :], raw[:, c, :], w_hi[:, 2 * par + c, :].bitcast(F32),
                                           ALU.subtract).then_inc(lo_ready, 1)

                    def stage_v(p):
                        pool.tensor_copy(diag[:, :, :], vt[:, :, bass.ds(p * P, P)]).then_inc(vp_copied, 1)
                        pool.wait_ge(vp_copied, p + 1)
                        pool.tensor_tensor(vp_hi[:, :, :], diag[:, :, :],
                                           ones[:, :].rearrange("p (a n) -> p a n", a=1).broadcast_to([P, TT, P]),
                                           ALU.mult).then_inc(vp_ready, 1)
                        pool.wait_ge(vp_ready, 2 * p + 1)
                        pool.tensor_tensor(vp_lo[:, :, :], diag[:, :, :], vp_hi[:, :, :].bitcast(F32),
                                           ALU.subtract).then_inc(vp_ready, 1)

                    def head_pair(p, par):
                        for e in range(2):
                            split_unit(p + (b + 8), (b + par) % 2, e)
                        pool.wait_ge(o_ready, 2 * p + 2)
                        stage_v(p + 1)

                    pool.wait_ge(v_ready, 4 * TT)
                    stage_v(0)
                    with pool.Fori(0, 3) as i:
                        head_pair(2 * i, 0)
                        head_pair(2 * i + 1, 1)
                    pool.wait_ge(o_ready, 14)
                    stage_v(7)
                post(s)

        @block.scalar
        def _(act):
            def split(pair, par):
                for c in range(2):
                    split_unit(pair, par, c)

            def split_unit(pair, par, c):
                act.wait_ge(raw_loaded[c], 16 * pair + 16)
                if not (isinstance(pair, int) and pair < 2):
                    act.wait_ge(w_used, 2 * pair + (c - 3))
                act.activation(w_hi[:, 2 * par + c, :], raw[:, c, :], ACT.Copy).then_inc(hi_ready, 1)

            def stat(t, scale, bias, src):
                act.activation(std[:, t % 2, :], src, ACT.Sqrt, bias=bias, scale=scale).then_inc(std_ready, 1)

            def pre_hi(s, d):
                act.wait_ge(h_ready, 8 * s + d + 1)
                act.activation(xn_hi[:, d, :], h[:, d, :], ACT.Copy, scale=gain(True, s, d)).then_inc(xhi_ready, 1)

            def pre_squares(s):
                for d in range(KC):
                    act.wait_ge(h_ready, 8 * s + d + 1)
                    act.activation(m[:, d, :], h[:, d, :], ACT.Square).then_inc(hsq_ready, 1)

            def pre_stat(s):
                act.wait_ge(ss_ready, 2 * s + 1)
                stat(2 * s, 1.0 / DM, eps_col[:, 0:1], bank[2][:, 0:TT])

            def out_square(s, d):
                act.wait_ge(m_evac, 8 * s + d + 1)
                act.activation(sq[:, d, :], m[:, d, :], ACT.Square).then_inc(msq_ready, 1)

            def post(s):
                act.preload_act_table(ACT.Sqrt)
                if SUBS[s][0] != "attn":
                    for d in range(KC):
                        out_square(s, d)
                act.wait_ge(s_ready, s + 1)
                stat(2 * s + 1, 4.0 if SUBS[s][0] == "ffn" else 1.0, 0.0, s_tok[:, :])

            def boundary(s):
                b = BASE[s]
                if s:
                    split_unit(b + 1, (b + 1) % 2, 0)
                for d in range(KC):
                    pre_hi(s, d)
                if s:
                    split_unit(b + 1, (b + 1) % 2, 1)
                pre_squares(s)
                split(b + 2, b % 2)
                pre_stat(s)

            act.wait_ge(gains_ready, 1)
            split(0, 0)
            split(1, 1)

            for s, (kind, _, _) in enumerate(SUBS):
                b = BASE[s]
                boundary(s)
                if kind == "ffn":
                    q0 = NF * ffn_index(s)

                    def hidden(f, c, pair):
                        if pair is not None:
                            split_unit(pair, (b + c) % 2, 0)
                        act.wait_ge(t1_ready, q0 + f + 1)
                        act.activation(t1[:, c, :], t1[:, c, :], ACT.Silu).then_inc(silu_ready, 1)
                        if pair is not None:
                            split_unit(pair, (b + c) % 2, 1)
                        act.wait_ge(y_ready, q0 + f + 1)
                        act.activation(hid_hi[:, bass.ds(f, 1), :], yf[:, c:c + 1, :], ACT.Copy).then_inc(hid_hi_ready, 1)

                    hidden(0, 0, None)
                    hidden(1, 1, b + 3)
                    with act.Fori(1, NF // 2) as i:
                        for c in range(2):
                            hidden(2 * i + c, c, 2 * i + (b + c + 2))
                    last = s == NSUB - 1
                    with act.Fori(0, 4 if last else 5) as i:
                        for c in range(2):
                            split(2 * i + (b + NF + c + 2), (b + c) % 2)
                    if last:
                        split(b + NF + 10, b % 2)
                if kind == "gmlp":
                    def v_gelu(c):
                        act.wait_ge(w_used, 2 * b + (4 if c == 0 else 10))
                        act.wait_ge(rstd_ready, 2 * s + 1)
                        for tt in range(TT):
                            act.activation(v[:, tt, c * T:(c + 1) * T], bank[4 + tt][:, :], ACT.Gelu,
                                           scale=rstd[:, 0, tt:tt + 1],
                                           accum_out=vst[:, 4 * c + tt:4 * c + tt + 1]).then_inc(v_ready, 1)

                    def u_gelu(i):
                        for c in range(2):
                            act.wait_ge(ut_ready, 2 * i + c + 1)
                            act.activation(u[:, 2 * i + c, :], ut[:, c, :], ACT.Gelu).then_inc(u_ready, 1)

                    v_gelu(0)
                    split(b + 3, (b + 3) % 2)
                    u_gelu(0)
                    split(b + 4, b % 2)
                    split(b + 5, (b + 5) % 2)
                    v_gelu(1)
                    split(b + 6, b % 2)
                    act.wait_ge(ln_step, 2)
                    for tt in range(TT):
                        if tt:
                            act.wait_ge(ln_sq, tt)
                        act.activation(vsq[:, :], v[:, tt, :], ACT.Square, bias=vst[:, 12 + tt:13 + tt],
                                       accum_out=vst[:, 16 + tt:17 + tt]).then_inc(ln_sq, 1)
                    act.wait_ge(ln_sq, TT)
                    act.activation(vst[:, 20:24], vst[:, 16:20], ACT.Sqrt, bias=eps_col[:, 1:2],
                                   scale=1.0 / DM).then_inc(ln_std, 1)
                    act.wait_ge(ws_turned, 1)
                    for q in range(2):
                        act.activation(wsT[:, 4 * q:4 * q + 4, :], bank[4 + q][:, :].rearrange("p (g t) -> p g t", g=4),
                                       ACT.Copy).then_inc(ws_ready, 1)

                    def y_high(g):
                        act.wait_ge(ym_ready, g + 1)
                        act.activation(y_hi[:, g, :], yt[:, g % 2, :], ACT.Copy).then_inc(yhi_ready, 1)

                    u_gelu(1)
                    split(b + 7, (b + 7) % 2)
                    u_gelu(2)
                    split(b + 8, b % 2)
                    y_high(0)
                    y_high(1)
                    u_gelu(3)
                    split(b + 9, (b + 9) % 2)
                    for g in range(2, G):
                        y_high(g)
                    split(b + 10, b % 2)
                    split(b + 11, (b + 11) % 2)
                    split(b + 12, b % 2)
                if kind == "attn":
                    def v_out(c):
                        act.wait_ge(w_used, 2 * b + (4 if c == 0 else 10))
                        act.wait_ge(rstd_ready, 2 * s + 1)
                        for tt in range(TT):
                            act.activation(vt[:, tt, c * T:(c + 1) * T], bank[4 + tt][:, :], ACT.Copy,
                                           scale=rstd[:, 0, tt:tt + 1]).then_inc(v_ready, 1)

                    def qk_high(p, par, c):
                        act.wait_ge(qy_ready, 2 * p + c + 1)
                        act.activation(qk_hi[:, par, c, :], qy[:, c, :], ACT.Copy,
                                       scale=QSCALE if c == 0 else 1.0).then_inc(qk_hi_ready, 1)

                    def keep_exp(n, e):
                        act.wait_ge(z_ready, n + 1)
                        if not (isinstance(n, int) and n < 2):
                            act.wait_ge(alo_ready, n - 1)
                        for p0, p1, s0, s1 in PIECES:
                            act.activation(e_t[:, e, s0:s1], psum[:, Z0[e] + p0:Z0[e] + p1], ACT.Abs).then_inc(e_step, 1)
                        act.wait_ge(e_step, 4 * n + 2)
                        act.activation(e_t[:, e, :], e_t[:, e, :], ACT.Exp, scale=-1.0).then_inc(e_step, 1)

                    def keep_ln(n, e):
                        act.wait_ge(e_step, 4 * n + 3)
                        act.activation(e_t[:, e, :], e_t[:, e, :], ACT.Ln, bias=ones[:, 0:1]).then_inc(e_step, 1)

                    def weights(n, e):
                        act.wait_ge(loga_ready, n + 1)
                        for p0, p1, s0, s1 in PIECES:
                            act.activation(e_t[:, e, s0:s1], psum[:, Z0[e] + p0:Z0[e] + p1], ACT.Exp).then_inc(a_ready, 1)

                    def head_out(n, p, e):
                        act.wait_ge(o_ready, n + 1)
                        rows = slice(HD * e, HD * e + HD)
                        act.activation(o_hi[rows, bass.ds(p, 1), :], bank[6][rows, :].rearrange("p (a n) -> p a n", a=1),
                                       ACT.Copy).then_inc(ohi_ready, 1)

                    def head_pair(p, par, more, last=False):
                        for e in range(2):
                            n = 2 * p + e
                            if not (last and e):
                                keep_exp(n + 1, 1 - e)
                            weights(n, e)
                            if not (last and e):
                                keep_ln(n + 1, 1 - e)
                            if more:
                                split_unit(p + (b + 8), (b + par) % 2, e)
                                qk_high(p + 2, par, e)
                            head_out(n, p, e)

                    v_out(0)
                    split(b + 3, (b + 3) % 2)
                    qk_high(0, 0, 0)
                    qk_high(0, 0, 1)
                    split(b + 4, b % 2)
                    split(b + 5, (b + 5) % 2)
                    v_out(1)
                    split(b + 6, b % 2)
                    act.preload_act_table_set("natural_log_exp_and_others")
                    keep_exp(0, 0)
                    keep_ln(0, 0)
                    qk_high(1, 1, 0)
                    qk_high(1, 1, 1)
                    split(b + 7, (b + 7) % 2)
                    head_pair(0, 0, True)
                    head_pair(1, 1, True)
                    with act.Fori(1, 3) as i:
                        head_pair(2 * i, 0, True)
                        head_pair(2 * i + 1, 1, True)
                    head_pair(6, 0, False)
                    head_pair(7, 1, False, last=True)
                    split(b + 14, b % 2)
                    out_square(s, 0)
                    out_square(s, 1)
                    split(b + 15, (b + 15) % 2)
                    for d in range(2, 5):
                        out_square(s, d)
                    for c in range(2):
                        split_unit(b + 16, b % 2, c)
                        out_square(s, 5 + c)
                    out_square(s, 7)
                post(s)
            for q in range(1, 2 * TT, 2):
                act.wait_ge(out_turned, q + 1)
                act.activation(o_tok[:, q // 2, T:2 * T], bank[q][:, :], ACT.Copy).then_inc(out_odd, 1)

        @block.vector
        def _(dve):
            def split_unit(pair, par, c):
                dve.wait_ge(hi_ready, 2 * pair + c + 1)
                dve.tensor_tensor(w_lo[:, 2 * par + c, :], raw[:, c, :], w_hi[:, 2 * par + c, :].bitcast(F32),
                                  ALU.subtract).then_inc(lo_ready, 1)

            def split(pair, par):
                split_unit(pair, par, 0)
                split_unit(pair, par, 1)

            def pre_lo(s, d):
                dve.wait_ge(xhi_ready, 8 * s + d + 1)
                dve.scalar_tensor_tensor(out=xn_lo[:, d, :], in0=h[:, d, :], scalar=gain(True, s, d),
                                         in1=xn_hi[:, d, :].bitcast(F32), op0=ALU.mult,
                                         op1=ALU.subtract).then_inc(xlo_ready, 1)

            def root(t):
                dve.wait_ge(std_ready, t + 1)
                dve.reciprocal(rstd[:, t % 2, :], std[:, t % 2, :]).then_inc(rstd_ready, 1)
                dve.wait_ge(rstd_ready, t + 1)
                for tt in range(TT):
                    last = dve.tensor_scalar(diag[:, tt, :], ident[:, :], rstd[:, t % 2, tt:tt + 1], None, ALU.mult)
                last.then_inc(diag_ready, 1)

            def pre_rest(s):
                dve.wait_ge(hsq_ready, 8 * s + 4)
                dve.tensor_tensor(sqb[:, :], m[:, 1, :], m[:, 3, :], ALU.add).then_inc(hsum_odd, 1)
                for i, d in enumerate((5, 7)):
                    dve.wait_ge(hsq_ready, 8 * s + d + 1)
                    dve.wait_ge(hsum_odd, 3 * s + i + 1)
                    dve.tensor_tensor(sqb[:, :], sqb[:, :], m[:, d, :], ALU.add).then_inc(hsum_odd, 1)
                b = BASE[s]
                split(b + 2, b % 2)
                root(2 * s)
                if SUBS[s][0] == "ffn":
                    dve.scalar_tensor_tensor(out=e2[:, :], in0=std[:, 0, :], scalar=RMS_EPS, in1=std[:, 0, :],
                                             op0=ALU.mult, op1=ALU.mult).then_inc(e2_ready, 1)
                else:
                    dve.memset(e2[:, :], RMS_EPS).then_inc(e2_ready, 1)
                dve.wait_ge(bc_ready, 2 * s + 1)
                dve.tensor_copy(rbc[:, :], bank[3][:, :]).then_inc(rbc_ready, 1)

            def out_evac(s, d):
                if SUBS[s][0] == "attn":
                    dve.wait_ge(w_used, 2 * (BASE[s + 1] - 4) + d + 1)
                elif d < KC - 1:
                    dve.wait_ge(acc_done, acc_base(s) + d + 1)
                else:
                    dve.wait_ge(w_used, 2 * BASE[s + 1])
                if SUBS[s][0] == "attn" and d < EARLY:
                    dve.wait_ge(part_ready, EARLY)
                    dve.tensor_tensor(m[:, d, :], bank[d][:, :], part[:, d, :], ALU.add).then_inc(m_evac, 1)
                else:
                    dve.tensor_copy(m[:, d, :], bank[d][:, :]).then_inc(m_evac, 1)

            def post(s):
                if SUBS[s][0] != "attn":
                    for d in range(KC):
                        out_evac(s, d)
                dve.wait_ge(ss_ready, 2 * s + 2)
                dve.wait_ge(e2_ready, s + 1)
                dve.scalar_tensor_tensor(out=s_tok[:, :], in0=bank[0][:, 0:TT], scalar=1.0 / DM, in1=e2[:, :],
                                         op0=ALU.mult, op1=ALU.add).then_inc(s_ready, 1)
                root(2 * s + 1)

            def apply(s, d):
                dve.scalar_tensor_tensor(out=m[:, d, :], in0=m[:, d, :], scalar=gain(False, s, d),
                                         in1=bank[1][:, :], op0=ALU.mult, op1=ALU.mult).then_inc(applied, 1)

            def add_own(s, d):
                dve.wait_ge(applied, 8 * s + d + 1)
                dve.tensor_tensor(h[:, d, :], h[:, d, :], m[:, d, :], ALU.add).then_inc(h_ready, 1)

            def boundary(s):
                b = BASE[s]
                if s:
                    split_unit(b + 1, (b + 1) % 2, 0)
                    dve.wait_ge(bc_ready, 2 * s)
                    LAG = 3
                    for d in range(KC + LAG):
                        if d < KC:
                            apply(s - 1, d)
                        if d < OWN_ADDS:
                            add_own(s - 1, d)
                        if d >= LAG:
                            pre_lo(s, d - LAG)
                    split_unit(b + 1, (b + 1) % 2, 1)
                else:
                    for d in range(KC):
                        pre_lo(s, d)
                pre_rest(s)

            dve.wait_ge(const_ready, 10)
            dve.tensor_copy(neg_tri[:, :], tri_f[:, 0, :]).then_inc(const2_ready, 1)
            dve.tensor_copy(neg_ones[:, :], tri_f[:, 1, :]).then_inc(const2_ready, 1)
            dve.tensor_copy(mask_bf[:, :], tri_f[:, 2:4, :].rearrange("p a n -> p (a n)")).then_inc(const2_ready, 1)
            dve.tensor_copy(ident_bf[:, :], ident[:, :]).then_inc(const2_ready, 1)
            dve.wait_ge(turned, 1)
            dve.tensor_copy(gcol[:, 0:NG], bank[0][:, 0:NG]).then_inc(gains_ready, 1)
            for d in range(KC):
                dve.wait_ge(turned, d + 2)
                dve.tensor_copy(h[:, d, :], bank[(d + 1) % KC][:, :]).then_inc(h_ready, 1)
            dve.wait_ge(gains_ready, 1)
            split(0, 0)
            split(1, 1)

            for s, (kind, _, _) in enumerate(SUBS):
                b = BASE[s]
                boundary(s)
                dve.wait_ge(rbc_ready, s + 1)
                if kind == "ffn":
                    q0 = NF * ffn_index(s)

                    def hidden(f, c, pair):
                        dve.wait_ge(w_used, 2 * f + (2 * b + 2))
                        dve.tensor_tensor(t1[:, c, :], bank[4 + 2 * c][:, :], rbc[:, :], ALU.mult).then_inc(t1_ready, 1)
                        if pair is not None:
                            split_unit(pair, (b + c) % 2, 0)
                        dve.wait_ge(silu_ready, q0 + f + 1)
                        dve.tensor_tensor(yf[:, c, :], bank[5 + 2 * c][:, :], t1[:, c, :], ALU.mult).then_inc(y_ready, 1)
                        if pair is not None:
                            split_unit(pair, (b + c) % 2, 1)
                        dve.wait_ge(hid_hi_ready, q0 + f + 1)
                        dve.tensor_tensor(hid_lo[:, bass.ds(f, 1), :], yf[:, c:c + 1, :],
                                          hid_hi[:, bass.ds(f, 1), :].bitcast(F32), ALU.subtract).then_inc(hid_lo_ready, 1)

                    hidden(0, 0, None)
                    hidden(1, 1, b + 3)
                    with dve.Fori(1, NF // 2) as i:
                        for c in range(2):
                            hidden(2 * i + c, c, 2 * i + (b + c + 2))
                    last = s == NSUB - 1
                    with dve.Fori(0, 4 if last else 5) as i:
                        for c in range(2):
                            split(2 * i + (b + NF + c + 2), (b + c) % 2)
                    if last:
                        split(b + NF + 10, b % 2)
                if kind == "gmlp":
                    def u_scale(i):
                        pair = b + (2 if i == 0 else 4 + i)
                        dve.wait_ge(w_used, 2 * pair + 2)
                        for c in range(2):
                            if i:
                                dve.wait_ge(u_ready, 2 * i + c - 1)
                            dve.tensor_tensor(ut[:, c, :], bank[2 * (i % 2) + c][:, :], rbc[:, :],
                                              ALU.mult).then_inc(ut_ready, 1)

                    def gate_u(g):
                        dve.wait_ge(sp_done, g + 1)
                        dve.wait_ge(gm_loaded, 32)
                        dve.scalar_tensor_tensor(
                            out=yt[:, g % 2, :].rearrange("p (c t) -> p c t", c=TT),
                            in0=bank[4 + g % 4][:, :].rearrange("p (c t) -> p c t", c=TT),
                            scalar=gcol[:, 12 * KC + g:12 * KC + g + 1],
                            in1=bias_bc[:, g:g + 1, :].broadcast_to([P, TT, P]),
                            op0=ALU.mult, op1=ALU.add).then_inc(yt_ready, 1)
                        dve.wait_ge(yt_ready, g + 1)
                        dve.wait_ge(u_ready, g + 1)
                        dve.tensor_tensor(yt[:, g % 2, :], yt[:, g % 2, :], u[:, g, :], ALU.mult).then_inc(ym_ready, 1)
                        dve.wait_ge(yhi_ready, g + 1)
                        dve.tensor_tensor(y_lo[:, g, :], yt[:, g % 2, :], y_hi[:, g, :].bitcast(F32),
                                          ALU.subtract).then_inc(ylo_ready, 1)

                    split(b + 3, (b + 3) % 2)
                    u_scale(0)
                    split(b + 4, b % 2)
                    split(b + 5, (b + 5) % 2)
                    split(b + 6, b % 2)
                    dve.wait_ge(v_ready, 2 * TT)
                    dve.tensor_tensor(vst[:, 8:12], vst[:, 0:4], vst[:, 4:8], ALU.add).then_inc(ln_step, 1)
                    dve.wait_ge(ln_step, 1)
                    dve.tensor_scalar(vst[:, 12:16], vst[:, 8:12], -1.0 / DM, None, ALU.mult).then_inc(ln_step, 1)
                    dve.wait_ge(ln_std, 1)
                    dve.reciprocal(vst[:, 24:28], vst[:, 20:24]).then_inc(ln_step, 1)
                    dve.wait_ge(ln_step, 3)
                    for tt in range(TT):
                        dve.tensor_scalar(v[:, tt, :], v[:, tt, :], vst[:, 12 + tt:13 + tt], vst[:, 24 + tt:25 + tt],
                                          ALU.add, ALU.mult).then_inc(vn_ready, 1)
                    u_scale(1)
                    split(b + 7, (b + 7) % 2)
                    u_scale(2)
                    split(b + 8, b % 2)
                    gate_u(0)
                    gate_u(1)
                    u_scale(3)
                    split(b + 9, (b + 9) % 2)
                    for g in range(2, G):
                        gate_u(g)
                    split(b + 10, b % 2)
                    split(b + 11, (b + 11) % 2)
                    split(b + 12, b % 2)
                if kind == "attn":
                    def qk_out(c, src):
                        dve.tensor_tensor(qy[:, c, :], src[:, :], rbc[:, :], ALU.mult).then_inc(qy_ready, 1)

                    def qk_low(p, par, c):
                        dve.wait_ge(qk_hi_ready, 2 * p + c + 1)
                        dve.scalar_tensor_tensor(
                            out=qk_lo[:, par, c, :], in0=qy[:, c, :], scalar=QSCALE if c == 0 else 1.0,
                            in1=qk_hi[:, par, c, :].bitcast(F32), op0=ALU.mult, op1=ALU.subtract).then_inc(qk_lo_ready, 1)

                    def keep(n, e, between=None):
                        dve.wait_ge(e_step, 4 * n + 4)
                        for p0, p1, s0, s1 in PIECES:
                            dve.scalar_tensor_tensor(out=e_t[:, e, s0:s1], in0=psum[:, Z0[e] + p0:Z0[e] + p1], scalar=0.0,
                                                     in1=e_t[:, e, s0:s1], op0=ALU.max, op1=ALU.add).then_inc(sp_ready, 1)
                        dve.wait_ge(sp_ready, 2 * n + 2)
                        if not (isinstance(n, int) and n < 2):
                            dve.wait_ge(o_ready, n - 1)
                        dve.tensor_copy(p_hi[:, e, :], e_t[:, e, :]).then_inc(sphi_ready, 1)
                        if between:
                            between()
                        dve.wait_ge(sphi_ready, n + 1)
                        dve.tensor_tensor(p_lo[:, e, :], e_t[:, e, :], p_hi[:, e, :].bitcast(F32),
                                          ALU.subtract).then_inc(splo_ready, 1)

                    def weights(n, e):
                        dve.wait_ge(a_ready, 2 * n + 2)
                        dve.tensor_copy(p_hi[:, e, :], e_t[:, e, :]).then_inc(ahi_ready, 1)
                        dve.wait_ge(ahi_ready, n + 1)
                        dve.tensor_tensor(p_lo[:, e, :], e_t[:, e, :], p_hi[:, e, :].bitcast(F32),
                                          ALU.subtract).then_inc(alo_ready, 1)

                    def head_out(n, p, e):
                        dve.wait_ge(ohi_ready, n + 1)
                        rows = slice(HD * e, HD * e + HD)
                        dve.tensor_tensor(o_lo[rows, bass.ds(p, 1), :], bank[6][rows, :].rearrange("p (a n) -> p a n", a=1),
                                          o_hi[rows, bass.ds(p, 1), :].bitcast(F32), ALU.subtract).then_inc(olo_ready, 1)

                    def head_pair(p, par, more, last=False):
                        for e in range(2):
                            n = 2 * p + e
                            weights(n, e)

                            def project_out():
                                if more:
                                    dve.wait_ge(w_used, 2 * p + (2 * b + 13 + e))
                                    qk_out(e, bank[7])
                                else:
                                    d = n - (2 * HEAD_PAIRS - EARLY)
                                    dve.wait_ge(part_done, d + 1)
                                    dve.tensor_copy(part[:, d, :], bank[7][:, :]).then_inc(part_ready, 1)

                            if last and e:
                                project_out()
                            else:
                                keep(n + 1, 1 - e, project_out)
                            if more:
                                qk_low(p + 2, par, e)
                            head_out(n, p, e)

                    split(b + 3, (b + 3) % 2)
                    dve.wait_ge(w_used, 2 * b + 6)
                    for c in range(2):
                        qk_out(c, bank[c])
                        qk_low(0, 0, c)
                    split(b + 4, b % 2)
                    split(b + 5, (b + 5) % 2)
                    split(b + 6, b % 2)
                    keep(0, 0)
                    dve.wait_ge(w_used, 2 * b + 12)
                    for c in range(2):
                        qk_out(c, bank[3 + 4 * c])
                        qk_low(1, 1, c)
                    split(b + 7, (b + 7) % 2)
                    head_pair(0, 0, True)
                    head_pair(1, 1, True)
                    with dve.Fori(1, 3) as i:
                        head_pair(2 * i, 0, True)
                        head_pair(2 * i + 1, 1, True)
                    head_pair(6, 0, False)
                    head_pair(7, 1, False, last=True)
                    dve.wait_ge(lo_ready, 2 * b + 28)
                    split(b + 14, b % 2)
                    out_evac(s, 0)
                    out_evac(s, 1)
                    split(b + 15, (b + 15) % 2)
                    for d in range(2, 5):
                        out_evac(s, d)
                    for c in range(2):
                        split_unit(b + 16, b % 2, c)
                        out_evac(s, 5 + c)
                    out_evac(s, 7)
                post(s)
            dve.wait_ge(bc_ready, 2 * NSUB)
            for d in range(KC):
                apply(NSUB - 1, d)
                if d < OWN_ADDS:
                    add_own(NSUB - 1, d)
            for q in range(0, 2 * TT, 2):
                dve.wait_ge(out_turned, q + 1)
                dve.tensor_copy(o_tok[:, q // 2, 0:T], bank[q][:, :]).then_inc(out_even, 1)

        @block.tensor
        def _(pe):
            def passes(dst, a_hi, a_lo, b_hi, b_lo, start, stop):
                pe.matmul(dst, a_hi, b_hi, start=start, stop=False)
                pe.matmul(dst, a_hi, b_lo, start=False, stop=False)
                return pe.matmul(dst, a_lo, b_hi, start=False, stop=stop)

            def split_ready(pair):
                pe.wait_ge(lo_ready, 2 * pair + 2)

            def ss(t, dst, parts):
                for i, part in enumerate(parts):
                    if t % 2 and i:
                        pe.wait_ge(msq_ready, 8 * (t // 2) + 5 + i)
                    for tt in range(TT):
                        last = pe.matmul(dst[:, tt:tt + 1], part[:, tt * P:(tt + 1) * P], ones[:, 0:1],
                                         start=i == 0 and tt == 0, stop=i == len(parts) - 1, skip_group_check=True)
                last.then_inc(ss_ready, 1)

            def broadcast(t, dst):
                pe.wait_ge(diag_ready, t + 1)
                pe.matmul(dst[:, :], ones[:, :], diag[:, :, :].rearrange("p c t -> p (c t)"), start=True,
                          stop=True).then_inc(bc_ready, 1)

            def pre_ss(s):
                pe.wait_ge(hsum_even, 3 * s + 3)
                pe.wait_ge(hsum_odd, 3 * s + 3)
                ss(2 * s, bank[2], [sqa, sqb])

            def post_stats(s):
                pe.wait_ge(msum_done, 4 * s + 4)
                ss(2 * s + 1, bank[0], [sqa, sq[:, 5, :], sq[:, 6, :], sq[:, 7, :]])
                broadcast(2 * s + 1, bank[1])

            def columns_pair(s, par, pair, at, arriving=False, hooks=False):
                split_ready(pair)
                for k in range(KC):
                    w = slice(k * P, (k + 1) * P)
                    if arriving:
                        pe.wait_ge(xhi_ready, 8 * s + k + 1)
                        for c in range(2):
                            pe.matmul(bank[at + c][:, :], w_hi[:, 2 * par + c, w], xn_hi[:, k, :], start=k == 0, stop=False)
                            pe.matmul(bank[at + c][:, :], w_lo[:, 2 * par + c, w], xn_hi[:, k, :], start=False, stop=False)
                        pe.wait_ge(xlo_ready, 8 * s + k + 1)
                        for c in range(2):
                            last = pe.matmul(bank[at + c][:, :], w_hi[:, 2 * par + c, w], xn_lo[:, k, :], start=False,
                                             stop=k == KC - 1)
                    for c in range(0 if arriving else 2):
                        last = passes(bank[at + c][:, :], w_hi[:, 2 * par + c, w], w_lo[:, 2 * par + c, w],
                                      xn_hi[:, k, :], xn_lo[:, k, :], k == 0, k == KC - 1)
                    if k == KC - 1:
                        last.then_inc(w_used, 2)
                    if hooks and k == 3:
                        pre_ss(s)
                    if hooks and k == 6:
                        broadcast(2 * s, bank[3])

            def column_unit(par, c, dst):
                for k in range(KC):
                    w = slice(k * P, (k + 1) * P)
                    last = passes(dst[:, :], w_hi[:, 2 * par + c, w], w_lo[:, 2 * par + c, w],
                                  xn_hi[:, k, :], xn_lo[:, k, :], k == 0, k == KC - 1)
                last.then_inc(w_used, 1)

            def tokens_pair(s, pair, half, arriving):
                split_ready(pair)
                par = pair % 2
                for c in range(2):
                    for kk in range(2):
                        k = 4 * half + 2 * c + kk
                        if arriving:
                            pe.wait_ge(xhi_ready, 8 * s + k + 1)
                            pe.wait_ge(xlo_ready, 8 * s + k + 1)
                        for tt in range(TT):
                            tk = slice(tt * P, (tt + 1) * P)
                            w = slice(kk * T, (kk + 1) * T)
                            last = passes(bank[4 + tt][:, :], xn_hi[:, k, tk], xn_lo[:, k, tk],
                                          w_hi[:, 2 * par + c, w], w_lo[:, 2 * par + c, w], k == 0, k == KC - 1)
                    last.then_inc(w_used, 1)

            def project_unit(par, c, x_hi, x_lo, start, bank_wait=None):
                for d in range(KC):
                    if bank_wait:
                        bank_wait(d)
                    w = slice(d * P, (d + 1) * P)
                    last = passes(bank[d][:, :], w_hi[:, 2 * par + c, w], w_lo[:, 2 * par + c, w], x_hi, x_lo,
                                  start, False)
                last.then_inc(w_used, 1)

            def project_last(par, x_hi, x_lo):
                for d in range(KC):
                    for c in range(2):
                        w = slice(d * P, (d + 1) * P)
                        last = passes(bank[d][:, :], w_hi[:, 2 * par + c, w], w_lo[:, 2 * par + c, w],
                                      x_hi[:, c, :], x_lo[:, c, :], False, c == 1)
                    if d < KC - 1:
                        last.then_inc(acc_done, 1)
                    else:
                        last.then_inc(w_used, 2)

            pe.wait_ge(const_ready, 10)
            pe.wait_ge(g_loaded, 48)
            pe.transpose(bank[0][:, 0:NG], g_rows[0:NG, :], ident[0:NG, 0:NG]).then_inc(turned, 1)
            pe.wait_ge(x_loaded, 16 * TT)
            for d in range(KC):
                if d == KC - 1:
                    pe.wait_ge(gains_ready, 1)
                for tt in range(TT):
                    last = pe.transpose(bank[(d + 1) % KC][:, tt * P:(tt + 1) * P], x_in[:, tt, d * P:(d + 1) * P],
                                        ident[:, :])
                last.then_inc(turned, 1)

            for s, (kind, _, _) in enumerate(SUBS):
                b = BASE[s]
                if kind == "ffn":
                    q0 = NF * ffn_index(s)
                    columns_pair(s, b % 2, b, 4, arriving=True)
                    columns_pair(s, (b + 1) % 2, b + 1, 6, hooks=True)
                    with pe.Fori(1, NF // 2) as i:
                        for c in range(2):
                            pe.wait_ge(y_ready, 2 * i + (q0 + c - 1))
                            columns_pair(s, (b + c) % 2, 2 * i + (b + c), 4 + 2 * c)

                    def hidden_free(d):
                        if d in (4, 6):
                            pe.wait_ge(y_ready, q0 + NF - 1 + (d == 6))

                    for f in range(4):
                        if f % 2 == 0:
                            split_ready(b + NF + f // 2)
                        pe.wait_ge(hid_lo_ready, q0 + f + 1)
                        project_unit((b + f // 2) % 2, f % 2, hid_hi[:, f, :], hid_lo[:, f, :], f == 0,
                                     hidden_free if f == 0 else None)
                    with pe.Fori(1, 5) as i:
                        for c in range(2):
                            split_ready(2 * i + (b + NF + c))
                            for e in range(2):
                                pe.wait_ge(hid_lo_ready, 4 * i + (q0 + 2 * c + e + 1))
                                project_unit((b + c) % 2, e, hid_hi[:, bass.ds(4 * i + (2 * c + e), 1), :],
                                             hid_lo[:, bass.ds(4 * i + (2 * c + e), 1), :], False)
                    pe.wait_ge(hid_lo_ready, q0 + NF)
                    split_ready(b + NF + NF // 2 - 1)
                    project_last((b + NF // 2 - 1) % 2, hid_hi[:, NF - 2:NF, :], hid_lo[:, NF - 2:NF, :])
                if kind == "gmlp":
                    tokens_pair(s, b, 0, True)
                    tokens_pair(s, b + 1, 1, True)
                    columns_pair(s, b % 2, b + 2, 0, hooks=True)
                    pe.wait_ge(v_ready, TT)
                    tokens_pair(s, b + 3, 0, False)
                    tokens_pair(s, b + 4, 1, False)
                    pe.wait_ge(rbc_ready, s + 1)
                    columns_pair(s, (b + 5) % 2, b + 5, 2)
                    pe.wait_ge(v_ready, 2 * TT)
                    pe.wait_ge(ws_masked, 1)
                    for g in range(G):
                        last = pe.transpose(bank[4 + g // 4][:, (g % 4) * P:(g % 4 + 1) * P], ws_raw[:, g, :], ident[:, :])
                    last.then_inc(ws_turned, 1)
                    pe.wait_ge(ut_ready, 2)
                    columns_pair(s, b % 2, b + 6, 0)

                    def mix(g):
                        if g >= 4:
                            pe.wait_ge(yt_ready, g - 3)
                        for c in range(TT):
                            last = pe.matmul(bank[4 + g % 4][:, c * P:(c + 1) * P], v[:, c, g * P:(g + 1) * P],
                                             wsT[:, g, :], start=True, stop=True)
                        last.then_inc(sp_done, 1)

                    pe.wait_ge(ws_ready, 2)
                    pe.wait_ge(vn_ready, TT)
                    mix(0)
                    mix(1)
                    pe.wait_ge(ut_ready, 4)
                    columns_pair(s, (b + 7) % 2, b + 7, 2)
                    for g in range(2, G):
                        mix(g)
                    pe.wait_ge(ut_ready, 8)

                    def mixed_free(d):
                        if d >= 4:
                            pe.wait_ge(yt_ready, d + 1)

                    for k in range(6):
                        if k % 2 == 0:
                            split_ready(b + 8 + k // 2)
                        pe.wait_ge(ylo_ready, k + 1)
                        project_unit((b + k // 2) % 2, k % 2, y_hi[:, k, :], y_lo[:, k, :], k == 0,
                                     mixed_free if k == 0 else None)
                    split_ready(b + 11)
                    pe.wait_ge(ylo_ready, KC)
                    project_last((b + 11) % 2, y_hi[:, 6:8, :], y_lo[:, 6:8, :])
                if kind == "attn":
                    tokens_pair(s, b, 0, True)
                    tokens_pair(s, b + 1, 1, True)
                    columns_pair(s, b % 2, b + 2, 0, hooks=True)
                    pe.wait_ge(v_ready, 3 * TT)
                    tokens_pair(s, b + 3, 0, False)
                    tokens_pair(s, b + 4, 1, False)
                    pe.wait_ge(const2_ready, 4)
                    pe.wait_ge(rbc_ready, s + 1)

                    def scores(n, e, par):
                        if not (isinstance(n, int) and n < 2):
                            pe.wait_ge(a_ready, 2 * n - 2)
                        rows = slice(HD * e, HD * e + HD)
                        for i in range(TT):
                            keys = slice(P * i, P * i + P)
                            q = slice(BQ[i], T)
                            at, col = BPOS[i]
                            dst = bank[3 * e + at][:, col:col + T - BQ[i]]
                            k_hi, k_lo = qk_hi[rows, par, 1, keys], qk_lo[rows, par, 1, keys]
                            q_hi, q_lo = qk_hi[rows, par, 0, q], qk_lo[rows, par, 0, q]
                            pe.matmul(dst, k_hi, q_hi, start=i < 3, stop=False, skip_group_check=i == 3)
                            pe.matmul(dst[:, 0:P * (1 + (i == 3))], ident_bf[:, :], mask_bf[:, P * (i < 3):2 * P],
                                      start=False, stop=False, skip_group_check=True)
                            pe.matmul(dst, k_hi, q_lo, start=False, stop=False, skip_group_check=i == 3)
                            last = pe.matmul(dst, k_lo, q_hi, start=False, stop=True, skip_group_check=i == 3)
                        last.then_inc(z_ready, 1)

                    def log_weights(n, e):
                        pe.wait_ge(splo_ready, n + 1)
                        for i in range(TT):
                            at, col = BPOS[i]
                            for c in range(i, TT):
                                dst = bank[3 * e + at][:, col + BQ[c] - BQ[i]:col + T - BQ[i]]
                                lhs = neg_tri if c == i else neg_ones
                                for part in (p_hi, p_lo):
                                    last = pe.matmul(dst, lhs[:, :], part[:, e, BOFF[c]:BOFF[c] + T - BQ[c]], start=False,
                                                     stop=True, skip_group_check=True)
                        last.then_inc(loga_ready, 1)

                    def weighted(n, p, e):
                        pe.wait_ge(alo_ready, n + 1)
                        pe.wait_ge(vp_ready, 2 * p + 2)
                        if not (isinstance(n, int) and n == 0):
                            pe.wait_ge(olo_ready, n)
                        for i in range(TT):
                            cols = slice(BOFF[i], BOFF[i] + T - BQ[i])
                            last = passes(bank[6][:, BQ[i]:T], vp_hi[:, i, :], vp_lo[:, i, :],
                                          p_hi[:, e, cols], p_lo[:, e, cols], i == 0, i == TT - 1)
                        last.then_inc(o_ready, 1)

                    def from_heads(par, c, dst, k, start, stop):
                        w = slice(k * P, (k + 1) * P)
                        return passes(dst[:, :], w_hi[:, 2 * par + c, w], w_lo[:, 2 * par + c, w],
                                      o_hi[:, k, :], o_lo[:, k, :], start, stop)

                    def done_pairs(d):
                        return (2 * HEAD_PAIRS - EARLY + d) // 2

                    def early_output(n, par, c):
                        d = n - (2 * HEAD_PAIRS - EARLY)
                        split_ready(b + 12 + d // 2)
                        pe.wait_ge(olo_ready, 2 * done_pairs(d))
                        if d == 0:
                            pe.wait_ge(qy_ready, 2 * HEAD_PAIRS)
                        else:
                            pe.wait_ge(part_ready, d)
                        for k in range(done_pairs(d)):
                            last = from_heads((b + par) % 2, c, bank[7], k, k == 0, k == done_pairs(d) - 1)
                        last.then_inc(part_done, 1)

                    def head_pair(p, par, more, last=False):
                        for e in range(2):
                            n = 2 * p + e
                            if not (last and e):
                                if e:
                                    pe.wait_ge(qk_lo_ready, 2 * p + 4)
                                scores(n + 1, 1 - e, par if e == 0 else 1 - par)
                            log_weights(n, e)
                            if more:
                                if e == 0:
                                    split_ready(p + (b + 6))
                                pe.wait_ge(qy_ready, 2 * p + 4 + e)
                                column_unit((b + par) % 2, e, bank[7])
                            else:
                                early_output(n, par, e)
                            weighted(n, p, e)

                    pe.wait_ge(qk_lo_ready, 2)
                    scores(0, 0, 0)
                    split_ready(b + 5)
                    pe.wait_ge(v_ready, 4 * TT)
                    column_unit((b + 5) % 2, 0, bank[3])
                    column_unit((b + 5) % 2, 1, bank[7])
                    pe.wait_ge(qy_ready, 4)
                    head_pair(0, 0, True)
                    head_pair(1, 1, True)
                    with pe.Fori(1, 3) as i:
                        head_pair(2 * i, 0, True)
                        head_pair(2 * i + 1, 1, True)
                    head_pair(6, 0, False)
                    head_pair(7, 1, False, last=True)
                    for d in range(2):
                        from_heads(b % 2, d, bank[d], 6, True, False)
                    pe.wait_ge(olo_ready, 2 * HEAD_PAIRS)
                    for d in range(EARLY):
                        from_heads((b + d // 2) % 2, d % 2, bank[d], 7, d >= 2, True).then_inc(w_used, 1)
                    pe.wait_ge(part_ready, EARLY)
                    for d in range(EARLY, KC):
                        pe.wait_ge(lo_ready, 2 * (b + 12) + d + 1)
                        for k in range(KC):
                            last = from_heads((b + d // 2) % 2, d % 2, bank[d], k, k == 0, k == KC - 1)
                        last.then_inc(w_used, 1)
                post_stats(s)
            pe.wait_ge(h_ready, 8 * NSUB + 8)
            for q in range(2 * TT):
                for c in range(4):
                    last = pe.transpose(bank[q][:, c * P:(c + 1) * P],
                                        h[:, 4 * (q % 2) + c, (q // 2) * P:(q // 2 + 1) * P], ident[:, :])
                last.then_inc(out_turned, 1)


_INS = ["x", "norm_pre", "norm_post", "ffn_w_gate", "ffn_w_up", "ffn_w_down", "a_w_in", "a_ln_g", "a_w_s",
        "a_b_s", "a_w_out", "b_w_qkv", "b_w_o"]


def kernel(**inputs):
    import numpy as _np
    import concourse.bacc as _bacc
    from concourse import mybir as _mybir
    from concourse.bass_utils import run_bass_kernel_spmd as _run

    nc = _bacc.Bacc("TRN2", target_bir_lowering=False, num_devices=1)
    arrays, args = {}, []
    for name in _INS:
        a = _np.ascontiguousarray(inputs[name])
        arrays[f"in_{name}_dram"] = a
        args.append(nc.dram_tensor(f"in_{name}_dram", a.shape, _mybir.dt.from_np(a.dtype), kind="ExternalInput").ap())
    args.append(nc.dram_tensor("out_dram", (1, T, DM), F32, kind="ExternalOutput").ap())
    build(nc, *args)
    r = _run(nc, [arrays], core_ids=[0])
    return r.results[0]["out_dram"]
```

```python
from contextlib import ExitStack

import concourse.bass as bass
from concourse import mybir
from concourse.alu_op_type import AluOpType as ALU

ACT = mybir.ActivationFunctionType
F32 = mybir.dt.float32
F32R = mybir.dt.float32r
BF16 = mybir.dt.bfloat16

P = 128
DM = 1024
KC = DM // P
T = 512
TT = T // P
DFF = 2816
NF = DFF // P
UNIT = 1024
G = 8
RMS_EPS = 1e-6
LN_EPS = 1e-5
HD = 64
HEAD_PAIRS = 8
QSCALE = HD ** -0.5
MASKED = -1e30

BQ = [0, 128, 256, 256]
BOFF = [0, 512, 896, 1152]
BPOS = [(0, 0), (1, 128), (2, 0), (2, 256)]
AW = 1408
PIECES = [(0, 512, 0, 512), (640, 1536, 512, 1408)]

SUBS = [("ffn", 0, 0), ("gmlp", 0, 0), ("ffn", 0, 1), ("ffn", 1, 0), ("attn", 0, 0), ("ffn", 1, 1)]
PAIRS = {"ffn": NF + NF // 2, "gmlp": 12, "attn": 16}
BASE = [sum(PAIRS[k] for k, _, _ in SUBS[:s]) for s in range(len(SUBS) + 1)]
NPAIR = BASE[-1]
NSUB = len(SUBS)
EARLY = 4
ORDER = "S0 S1 L0 S2 L1 S3 S4 L2 S5 L3 S6 L4 S7 L5 L6 L7".split()
SUMMED = [7, 5]
HALF = [slice(0, T // 2), slice(T // 2, T)]
A, B = 0, 1


def build(nc, x, norm_pre, norm_post, w_gate, w_up, w_down, a_w_in, a_ln_g, a_w_s, a_b_s, a_w_out,
          b_w_qkv, b_w_o, out):
    ctx = ExitStack()
    with ctx:
        cursor = [(nc.sbuf_base + 31) // 32 * 32]

        def place(name, shape, dt=F32, at=None):
            n = (4 if dt != BF16 else 2)
            for d in shape[1:]:
                n *= d
            if at is None:
                at = cursor[0]
                cursor[0] += (n + 31) // 32 * 32
            return nc.alloc_sbuf_tensor_at(name, shape, dt, offset=at), at + n

        def sb(name, shape, dt=F32):
            return place(name, shape, dt)[0]

        h = sb("h", [P, KC, T])
        xn_hi = sb("xn_hi", [P, KC, T], F32R)
        xn_lo = sb("xn_lo", [P, KC, T], F32R)
        raw = sb("raw", [P, 2, UNIT])
        w_hi = sb("w_hi", [P, 4, UNIT], F32R)
        w_lo = sb("w_lo", [P, 4, UNIT], F32R)
        sqa_at = cursor[0]
        sqa = sb("sqa", [P, T])
        sqb_at = cursor[0]
        sqb = sb("sqb", [P, T])
        diag = sb("diag", [P, TT, P])
        rbc = sb("rbc", [P, T])
        ident = sb("ident", [P, P])
        ones = sb("ones", [P, P])
        neg_tri = sb("neg_tri", [P, P], F32R)
        neg_ones = sb("neg_ones", [P, P], F32R)
        ident_bf = sb("ident_bf", [P, P], BF16)
        mask_bf = sb("mask_bf", [P, 2 * P], BF16)
        NG = 12 * KC + KC
        gcol = sb("gcol", [P, NG])
        std = sb("std", [P, TT])
        rstd = sb("rstd", [P, TT])
        e2 = sb("e2", [P, TT])
        m_mean = sb("m_mean", [P, TT])
        m_root = sb("m_root", [P, TT])
        m_inv = sb("m_inv", [P, TT])
        eps_col = sb("eps_col", [P, 2])

        region = cursor[0]
        m, after_m = place("m", [P, KC, T], at=region)
        sq, after_sq = place("sq", [P, KC, T], at=after_m)
        t1, a1 = place("t1", [P, 2, T], at=region)
        yf, _ = place("yf", [P, 2, T], at=a1)
        hid_hi, a1 = place("hid_hi", [P, NF, T], F32R, at=after_m)
        hid_lo, end_ffn = place("hid_lo", [P, NF, T], F32R, at=a1)
        u, a1 = place("u", [P, KC, T], at=after_m)
        v, a1 = place("v", [P, TT, DM], at=a1)
        y_hi, a1 = place("y_hi", [P, KC, T], F32R, at=a1)
        y_lo, a1 = place("y_lo", [P, KC, T], F32R, at=a1)
        wsT, a1 = place("wsT", [P, G, P], at=a1)
        bias_bc, a1 = place("bias_bc", [P, G, P], at=a1)
        vst, a1 = place("vst", [P, 40], at=a1)
        ws_raw, _ = place("ws_raw", [P, G, P], at=region)
        ut, a1 = place("ut", [P, 2, T], at=region + 4096)
        vsq, _ = place("vsq", [P, DM], at=a1)
        yt, _ = place("yt", [P, 4, T], at=a1)
        e_t, a1 = place("e_t", [P, 2, AW], at=region)
        p_hi, a1 = place("p_hi", [P, 2, AW], F32R, at=a1)
        p_lo, a1 = place("p_lo", [P, 2, AW], F32R, at=a1)
        assert a1 >= after_sq
        o_hi, a1 = place("o_hi", [P, KC, T], F32R, at=a1)
        o_lo, a1 = place("o_lo", [P, KC, T], F32R, at=a1)
        vt, a1 = place("vt", [P, TT, DM], at=a1)
        qk_hi, a1 = place("qk_hi", [P, 2, 2, T], F32R, at=a1)
        qk_lo, a1 = place("qk_lo", [P, 2, 2, T], F32R, at=a1)
        qy, _ = place("qy", [P, 2, T], at=a1)
        part, end_attn = place("part", [P, EARLY, T], at=a1)
        vp_hi, _ = place("vp_hi", [P, TT, P], F32R, at=sqa_at)
        vp_lo, _ = place("vp_lo", [P, TT, P], F32R, at=sqb_at)
        x_in, _ = place("x_in", [P, TT, DM], at=after_m)
        g_rows, _ = place("g_rows", [P, P], at=after_m + 16384)
        tri_f, _ = place("tri_f", [P, 4, P], at=after_m + 20480)
        o_tok, _ = place("o_tok", [P, TT, DM], at=after_m)
        assert max(end_ffn, end_attn) <= nc.sbuf_usable_end, (end_ffn, end_attn, nc.sbuf_usable_end)

        psum = ctx.enter_context(nc.psum_tensor("psum", [P, 8 * T], F32))
        bank = [psum[:, i * T:(i + 1) * T] for i in range(8)]

        def sem(name):
            return ctx.enter_context(nc.semaphore(name))

        def halves(name):
            return [sem(name + "_a"), sem(name + "_b")]

        x_loaded = halves("x_loaded")
        g_loaded = sem("g_loaded")
        gm_loaded = sem("gm_loaded")
        const_ready = sem("const_ready")
        const2_ready = sem("const2_ready")
        gains_turned = sem("gains_turned")
        x_turned = halves("x_turned")
        gains_ready = sem("gains_ready")
        raw_loaded = [sem("raw_loaded0"), sem("raw_loaded1")]
        hi_ready = sem("hi_ready")
        lo_ready = sem("lo_ready")
        w_used = sem("w_used")
        acc_done = halves("acc_done")
        m_evac = halves("m_evac")
        msq_ready = halves("msq_ready")
        msum_ready = halves("msum_ready")
        mtotal_ready = halves("mtotal_ready")
        mmean_ready = halves("mmean_ready")
        mroot_ready = halves("mroot_ready")
        minv_ready = halves("minv_ready")
        mdiag_ready = halves("mdiag_ready")
        mbc_ready = halves("mbc_ready")
        applied = halves("applied")
        h_ready = halves("h_ready")
        xhi_ready = halves("xhi_ready")
        xlo_ready = halves("xlo_ready")
        hsq_ready = sem("hsq_ready")
        hsum_even = sem("hsum_even")
        hsum_odd = sem("hsum_odd")
        htotal_ready = sem("htotal_ready")
        std_ready = sem("std_ready")
        rstd_ready = sem("rstd_ready")
        hdiag_ready = sem("hdiag_ready")
        hbc_ready = sem("hbc_ready")
        rbc_ready = sem("rbc_ready")
        e2_ready = sem("e2_ready")
        t1_ready = sem("t1_ready")
        silu_ready = sem("silu_ready")
        y_ready = sem("y_ready")
        hid_hi_ready = sem("hid_hi_ready")
        hid_lo_ready = sem("hid_lo_ready")
        v_ready = sem("v_ready")
        ln_step = sem("ln_step")
        ln_sq = sem("ln_sq")
        ln_std = sem("ln_std")
        vn_ready = sem("vn_ready")
        ws_masked = sem("ws_masked")
        ws_turned = sem("ws_turned")
        ws_ready = sem("ws_ready")
        ut_ready = sem("ut_ready")
        u_ready = sem("u_ready")
        sp_done = sem("sp_done")
        yt_ready = sem("yt_ready")
        ym_ready = sem("ym_ready")
        yhi_ready = sem("yhi_ready")
        ylo_ready = sem("ylo_ready")
        vp_copied = sem("vp_copied")
        vp_ready = sem("vp_ready")
        qy_ready = sem("qy_ready")
        qk_hi_ready = sem("qk_hi_ready")
        qk_lo_ready = sem("qk_lo_ready")
        z_ready = sem("z_ready")
        e_step = sem("e_step")
        part_done = sem("part_done")
        part_ready = sem("part_ready")
        sp_ready = sem("sp_ready")
        sphi_ready = sem("sphi_ready")
        splo_ready = sem("splo_ready")
        loga_ready = sem("loga_ready")
        a_ready = sem("a_ready")
        ahi_ready = sem("ahi_ready")
        alo_ready = sem("alo_ready")
        o_ready = sem("o_ready")
        ohi_ready = sem("ohi_ready")
        olo_ready = sem("olo_ready")
        out_turned = sem("out_turned")
        out_by_act = sem("out_by_act")
        out_by_dve = sem("out_by_dve")
        stored = sem("stored")

        def own_adds(s):
            return 2 if s < NSUB - 1 else 4

        def gain(pre, s, d):
            _, layer, j = SUBS[s]
            j = {"ffn": 2 * j, "gmlp": 1, "attn": 1}[SUBS[s][0]]
            at = (0 if pre else 6 * KC) + (layer if SUBS[s][0] != "attn" else 1) * 3 * KC + j * KC + d
            return gcol[:, at:at + 1]

        def ffn_index(s):
            return sum(k == "ffn" for k, _, _ in SUBS[:s])

        def wait_out(eng, s, d, half):
            cut_before = sum(k != "attn" for k, _, _ in SUBS[:s])
            attn_before = s - cut_before
            if SUBS[s][0] == "attn":
                if half == A and d >= KC - 2:
                    eng.wait_ge(acc_done[A], KC * cut_before + d - (KC - 3))
                else:
                    eng.wait_ge(w_used, 2 * (BASE[s + 1] - 4) + d + 1)
            elif half == A:
                eng.wait_ge(acc_done[A], KC * cut_before + 2 * attn_before + d + 1)
            elif d < KC - 1:
                eng.wait_ge(acc_done[B], (KC - 1) * cut_before + d + 1)
            else:
                eng.wait_ge(w_used, 2 * BASE[s + 1])

        COLS = [slice(0, TT // 2), slice(TT // 2, TT)]
        RBANK = [3, 4]
        XBANK = [(4, 5, 6, 7), (2, 3, 4, 5)]
        HB = [0, 6]
        TURN = [5, 6, 7, 0, 1, 2, 3, 4]
        Z0 = [0, 3 * T]

        block = ctx.enter_context(nc.Block())

        @block.sync
        def _(sp):
            sp.dma_start(g_rows[0:48, :], norm_pre.rearrange("l j (c p) -> (l j c) p", p=P)).then_inc(g_loaded, 16)
            sp.dma_start(g_rows[48:96, :], norm_post.rearrange("l j (c p) -> (l j c) p", p=P)).then_inc(g_loaded, 16)
            sp.dma_start(g_rows[96:104, :], a_ln_g.rearrange("l (c p) -> (l c) p", p=P)).then_inc(g_loaded, 16)

            def load_x(half):
                for tt in (2 * half, 2 * half + 1):
                    sp.dma_start(x_in[:, tt, :], x[0, tt * P:(tt + 1) * P, :]).then_inc(x_loaded[half], 16)

            load_x(A)

            def load(n, par, src, view):
                if not (isinstance(n, int) and n < 2):
                    sp.wait_ge(lo_ready, n - 1)
                sp.dma_start(view(raw[:, par, :]), src).then_inc(raw_loaded[par], 16)

            def by_k(dst):
                return dst.rearrange("p (k f) -> p k f", k=KC)

            def by_half(dst):
                return dst.rearrange("p (k f) -> p k f", k=2)

            def flat(dst):
                return dst

            for s, (kind, layer, j) in enumerate(SUBS):
                n0 = 2 * BASE[s]
                if kind == "ffn":
                    gate = w_gate[layer, j].rearrange("(k p) f -> p k f", p=P)
                    up = w_up[layer, j].rearrange("(k p) f -> p k f", p=P)
                    first = 1 if s == 0 else 0
                    for f in range(first):
                        load(n0 + 2 * f, 0, gate[:, :, f * P:(f + 1) * P], by_k)
                        load(n0 + 2 * f + 1, 1, up[:, :, f * P:(f + 1) * P], by_k)
                        load_x(B)
                    with sp.Fori(first, NF) as f:
                        load(n0 + 2 * f, 0, gate[:, :, bass.ds(f * P, P)], by_k)
                        load(n0 + 2 * f + 1, 1, up[:, :, bass.ds(f * P, P)], by_k)
                    n1 = n0 + 2 * NF
                    with sp.Fori(0, NF // 2) as i:
                        for c in range(2):
                            load(n1 + 2 * i + c, c, w_down[layer, j, bass.ds((2 * i + c) * P, P), :], flat)
                    continue
                w = (a_w_in if kind == "gmlp" else b_w_qkv)[0].rearrange("(k p) n -> p k n", p=P)
                v0 = DM if kind == "gmlp" else 2 * DM
                n = n0

                def load_v(n, c):
                    for q in range(4):
                        load(n + q, q % 2, w[:, 2 * q:2 * q + 2, v0 + c * T:v0 + (c + 1) * T], by_half)

                if kind == "gmlp":
                    for e in range(2):
                        load(n0 + e, e, w[:, :, e * P:(e + 1) * P], by_k)
                    load_v(n0 + 2, 0)
                    for e in range(2):
                        load(n0 + 6 + e, e, w[:, :, (2 + e) * P:(3 + e) * P], by_k)
                    sp.wait_ge(w_used, n0 + 2)
                    sp.wait_ge(rbc_ready, s + 1)
                    sp.dma_start(ws_raw[:, :, :], a_w_s[0].rearrange("g t s -> t g s")).then_inc(gm_loaded, 16)
                    sp.dma_start(bias_bc[:, :, :].rearrange("p g t -> p (g t)"),
                                 a_b_s[0].rearrange("g t -> (g t)").partition_broadcast(P)).then_inc(gm_loaded, 16)
                    load_v(n0 + 8, 1)
                    for e in range(4, 8):
                        load(n0 + 8 + e, e % 2, w[:, :, e * P:(e + 1) * P], by_k)
                    n1 = n0 + 16
                else:
                    load(n0, 0, w[:, :, 0:P], by_k)
                    load(n0 + 1, 1, w[:, :, DM:DM + P], by_k)
                    load_v(n0 + 2, 0)
                    load(n0 + 6, 0, w[:, :, P:2 * P], by_k)
                    load(n0 + 7, 1, w[:, :, DM + P:DM + 2 * P], by_k)
                    load_v(n0 + 8, 1)
                    with sp.Fori(2, HEAD_PAIRS) as p:
                        load(n0 + 8 + 2 * p, 0, w[:, :, bass.ds(p * P, P)], by_k)
                        load(n0 + 9 + 2 * p, 1, w[:, :, bass.ds(p * P + DM, P)], by_k)
                    w_o = b_w_o[0].rearrange("(k p) n -> p k n", p=P)
                    with sp.Fori(0, KC // 2) as i:
                        for c in range(2):
                            load(n0 + 24 + 2 * i + c, c, w_o[:, :, bass.ds((2 * i + c) * P, P)], by_k)
                    continue
                with sp.Fori(0, KC // 2) as i:
                    for c in range(2):
                        load(n1 + 2 * i + c, c, a_w_out[0, bass.ds((2 * i + c) * P, P), :], flat)
            for tt in range(TT):
                sp.wait_ge(out_by_act, (2, 4, 5, 6)[tt])
                if tt >= TT // 2:
                    sp.wait_ge(out_by_dve, tt - 1)
                sp.dma_start(out[0, tt * P:(tt + 1) * P, :], o_tok[:, tt, :]).then_inc(stored, 16)
            sp.wait_ge(stored, 16 * TT)

        @block.gpsimd
        def _(pool):
            pool.memset(ident[:, :], 0.0).then_inc(const_ready, 1)
            pool.memset(ones[:, :], 1.0).then_inc(const_ready, 1)
            pool.memset(eps_col[:, 0:1], RMS_EPS).then_inc(const_ready, 1)
            pool.memset(eps_col[:, 1:2], LN_EPS).then_inc(const_ready, 1)
            pool.memset(tri_f[:, 0, :], -1.0).then_inc(const_ready, 1)
            pool.memset(tri_f[:, 1, :], -1.0).then_inc(const_ready, 1)
            pool.memset(tri_f[:, 2:4, :], MASKED).then_inc(const_ready, 1)
            pool.wait_ge(const_ready, 7)
            pool.affine_select(out=ident[:, :], in_=ident[:, :], compare_op=ALU.not_equal, fill=1.0,
                               base=0, pattern=[[-1, P]], channel_multiplier=1).then_inc(const_ready, 1)
            pool.affine_select(out=tri_f[:, 0, :], in_=tri_f[:, 0, :], compare_op=ALU.is_ge, fill=0.0,
                               base=0, pattern=[[-1, P]], channel_multiplier=1).then_inc(const_ready, 1)
            pool.affine_select(out=tri_f[:, 3, :], in_=tri_f[:, 3, :], compare_op=ALU.is_ge, fill=0.0,
                               base=0, pattern=[[-1, P]], channel_multiplier=1).then_inc(const_ready, 1)

            def pre_sums(s):
                pool.wait_ge(hsq_ready, 8 * s + 3)
                pool.tensor_tensor(sqa[:, :], m[:, 0, :], m[:, 2, :], ALU.add).then_inc(hsum_even, 1)
                for i, d in enumerate((4, 6)):
                    pool.wait_ge(hsq_ready, 8 * s + d + 1)
                    pool.wait_ge(hsum_even, 3 * s + i + 1)
                    pool.tensor_tensor(sqa[:, :], sqa[:, :], m[:, d, :], ALU.add).then_inc(hsum_even, 1)

            def post(s):
                for half in (A, B):
                    hs = HALF[half]
                    for i, d in enumerate(range(1, SUMMED[half])):
                        pool.wait_ge(msq_ready[half], 8 * s + d + 1)
                        if d > 1:
                            pool.wait_ge(msum_ready[half], (SUMMED[half] - 1) * s + i)
                        pool.tensor_tensor(sqa[:, hs], sqa[:, hs] if d > 1 else sq[:, 0, hs], sq[:, d, hs],
                                           ALU.add).then_inc(msum_ready[half], 1)
                for half in (A, B):
                    hs = HALF[half]
                    for d in range(own_adds(s), KC):
                        pool.wait_ge(applied[half], 8 * s + d + 1)
                        pool.tensor_tensor(h[:, d, hs], h[:, d, hs], m[:, d, hs], ALU.add).then_inc(h_ready[half], 1)

            for s, (kind, _, _) in enumerate(SUBS):
                pre_sums(s)
                if kind == "gmlp":
                    pool.wait_ge(gm_loaded, 32)
                    pool.affine_select(out=ws_raw[:, :, :], in_=ws_raw[:, :, :], compare_op=ALU.is_ge, fill=0.0,
                                       base=0, pattern=[[0, G], [-1, P]], channel_multiplier=1).then_inc(ws_masked, 1)
                if kind == "attn":
                    b = BASE[s]

                    def split_unit(pair, par, c):
                        pool.wait_ge(hi_ready, 2 * pair + c + 1)
                        pool.wait_ge(lo_ready, 2 * pair + c)
                        pool.tensor_tensor(w_lo[:, 2 * par + c, :], raw[:, c, :], w_hi[:, 2 * par + c, :].bitcast(F32),
                                           ALU.subtract).then_inc(lo_ready, 1)

                    def stage_v(p):
                        pool.tensor_copy(diag[:, :, :], vt[:, :, bass.ds(p * P, P)]).then_inc(vp_copied, 1)
                        pool.wait_ge(vp_copied, p + 1)
                        pool.tensor_tensor(vp_hi[:, :, :], diag[:, :, :],
                                           ones[:, :].rearrange("p (a n) -> p a n", a=1).broadcast_to([P, TT, P]),
                                           ALU.mult).then_inc(vp_ready, 1)
                        pool.wait_ge(vp_ready, 2 * p + 1)
                        pool.tensor_tensor(vp_lo[:, :, :], diag[:, :, :], vp_hi[:, :, :].bitcast(F32),
                                           ALU.subtract).then_inc(vp_ready, 1)

                    def head_pair(p, par):
                        for e in range(2):
                            split_unit(p + (b + 8), (b + par) % 2, e)
                        pool.wait_ge(o_ready, 2 * p + 2)
                        stage_v(p + 1)

                    pool.wait_ge(v_ready, 4 * TT)
                    stage_v(0)
                    with pool.Fori(0, 3) as i:
                        head_pair(2 * i, 0)
                        head_pair(2 * i + 1, 1)
                    pool.wait_ge(o_ready, 14)
                    stage_v(7)
                post(s)

        @block.scalar
        def _(act):
            def split(pair, par):
                for c in range(2):
                    split_unit(pair, par, c)

            def split_unit(pair, par, c):
                act.wait_ge(raw_loaded[c], 16 * pair + 16)
                if not (isinstance(pair, int) and pair < 2):
                    act.wait_ge(w_used, 2 * pair + (c - 3))
                act.activation(w_hi[:, 2 * par + c, :], raw[:, c, :], ACT.Copy).then_inc(hi_ready, 1)

            def pre_hi(s, d, half):
                act.wait_ge(h_ready[half], 8 * s + d + 1)
                act.activation(xn_hi[:, d, HALF[half]], h[:, d, HALF[half]], ACT.Copy,
                               scale=gain(True, s, d)).then_inc(xhi_ready[half], 1)

            def pre_squares(s):
                for d in range(KC):
                    act.activation(m[:, d, :], h[:, d, :], ACT.Square).then_inc(hsq_ready, 1)

            def pre_root(s):
                act.wait_ge(htotal_ready, s + 1)
                act.activation(std[:, :], bank[2][:, 0:TT], ACT.Sqrt, bias=eps_col[:, 0:1],
                               scale=1.0 / DM).then_inc(std_ready, 1)

            def out_square(s, d, half):
                src = m[:, d, HALF[half]]
                if half == A:
                    act.wait_ge(m_evac[A], 8 * s + d + 1)
                elif SUBS[s][0] == "attn" and d < KC - 2:
                    act.wait_ge(m_evac[B], d + 1)
                else:
                    src = bank[d][:, HALF[B]]
                act.activation(sq[:, d, HALF[half]], src, ACT.Square).then_inc(msq_ready[half], 1)

            def out_b(s, d):
                wait_out(act, s, d, B)
                act.activation(m[:, d, HALF[B]], bank[d][:, HALF[B]], ACT.Copy)
                out_square(s, d, B)

            def out_root(s, half):
                cols = COLS[half]
                if SUBS[s][0] == "ffn":
                    act.wait_ge(mmean_ready[half], ffn_index(s) + 1)
                    act.activation(m_root[:, cols], m_mean[:, cols], ACT.Sqrt, scale=4.0).then_inc(mroot_ready[half], 1)
                else:
                    act.wait_ge(mtotal_ready[half], s + 1)
                    act.activation(m_root[:, cols], bank[2][:, cols], ACT.Sqrt, bias=eps_col[:, 0:1],
                                   scale=1.0 / DM).then_inc(mroot_ready[half], 1)

            def post(s):
                act.preload_act_table(ACT.Sqrt)
                for d in range(KC - 2 if SUBS[s][0] == "attn" else 0, KC):
                    out_square(s, d, A)

            def boundary(s):
                last = s == NSUB
                t = s - 1
                first = KC - 2 if SUBS[t][0] == "attn" else 0

                def hi(d, half):
                    if not last:
                        pre_hi(s, d, half)

                for d in range(first, 3):
                    out_b(t, d)
                out_root(t, A)
                for d in range(max(first, 3), 6):
                    out_b(t, d)
                for i in range(2):
                    hi(i, A)
                    out_b(t, i + 6)
                for d in range(2, 6):
                    hi(d, A)
                out_root(t, B)
                for d in range(6, KC):
                    hi(d, A)
                if last:
                    return
                b = BASE[s]
                for d in range(KC):
                    hi(d, B)
                    if d == 3:
                        split_unit(b + 1, (b + 1) % 2, 0)
                split_unit(b + 1, (b + 1) % 2, 1)

            def start():
                for d in range(KC):
                    pre_hi(0, d, A)
                split(0, 0)
                for j in range(KC // 2):
                    act.wait_ge(x_turned[B], j + 1)
                    act.activation(h[:, 2 * j:2 * j + 2, HALF[B]],
                                   bank[XBANK[B][j]][:, :].rearrange("p (c t) -> p c t", c=2),
                                   ACT.Copy).then_inc(h_ready[B], 2)
                for d in range(KC):
                    pre_hi(0, d, B)
                split(1, 1)

            def pre_norm(s):
                pre_squares(s)
                split(BASE[s] + 2, BASE[s] % 2)
                pre_root(s)

            act.wait_ge(gains_ready, 1)

            for s, (kind, _, _) in enumerate(SUBS):
                b = BASE[s]
                if s:
                    boundary(s)
                else:
                    start()
                pre_norm(s)
                if kind == "ffn":
                    q0 = NF * ffn_index(s)

                    def hidden(f, c, pair):
                        if pair is not None:
                            split_unit(pair, (b + c) % 2, 0)
                        act.wait_ge(t1_ready, q0 + f + 1)
                        act.activation(t1[:, c, :], t1[:, c, :], ACT.Silu).then_inc(silu_ready, 1)
                        if pair is not None:
                            split_unit(pair, (b + c) % 2, 1)
                        act.wait_ge(y_ready, q0 + f + 1)
                        act.activation(hid_hi[:, bass.ds(f, 1), :], yf[:, c:c + 1, :], ACT.Copy).then_inc(hid_hi_ready, 1)

                    hidden(0, 0, None)
                    hidden(1, 1, b + 3)
                    with act.Fori(1, NF // 2) as i:
                        for c in range(2):
                            hidden(2 * i + c, c, 2 * i + (b + c + 2))
                    last = s == NSUB - 1
                    with act.Fori(0, 4 if last else 5) as i:
                        for c in range(2):
                            split(2 * i + (b + NF + c + 2), (b + c) % 2)
                    if last:
                        split(b + NF + 10, b % 2)
                if kind == "gmlp":
                    def v_gelu(c):
                        act.wait_ge(w_used, 2 * b + (6 if c == 0 else 12))
                        act.wait_ge(rstd_ready, s + 1)
                        for tt in range(TT):
                            act.activation(v[:, tt, c * T:(c + 1) * T], bank[4 + tt][:, :], ACT.Gelu,
                                           scale=rstd[:, tt:tt + 1],
                                           accum_out=vst[:, 4 * c + tt:4 * c + tt + 1]).then_inc(v_ready, 1)

                    def u_gelu(i):
                        for c in range(2):
                            act.wait_ge(ut_ready, 2 * i + c + 1)
                            act.activation(u[:, 2 * i + c, :], ut[:, c, :], ACT.Gelu).then_inc(u_ready, 1)

                    u_gelu(0)
                    split(b + 3, (b + 3) % 2)
                    v_gelu(0)
                    split(b + 4, b % 2)
                    u_gelu(1)
                    split(b + 5, (b + 5) % 2)
                    split(b + 6, b % 2)
                    v_gelu(1)
                    split(b + 7, (b + 7) % 2)
                    act.wait_ge(ln_step, 2)
                    for tt in range(TT):
                        if tt:
                            act.wait_ge(ln_sq, tt)
                        act.activation(vsq[:, :], v[:, tt, :], ACT.Square, bias=vst[:, 12 + tt:13 + tt],
                                       accum_out=vst[:, 16 + tt:17 + tt]).then_inc(ln_sq, 1)
                    act.wait_ge(ln_sq, TT)
                    act.activation(vst[:, 20:24], vst[:, 16:20], ACT.Sqrt, bias=eps_col[:, 1:2],
                                   scale=1.0 / DM).then_inc(ln_std, 1)
                    act.preload_act_table(ACT.Gelu)
                    act.wait_ge(ws_turned, 1)
                    for q in range(2):
                        act.activation(wsT[:, 4 * q:4 * q + 4, :], bank[4 + q][:, :].rearrange("p (g t) -> p g t", g=4),
                                       ACT.Copy).then_inc(ws_ready, 1)

                    def y_high(g):
                        act.wait_ge(ym_ready, g + 1)
                        act.activation(y_hi[:, g, :], yt[:, g % 4, :], ACT.Copy).then_inc(yhi_ready, 1)

                    u_gelu(2)
                    split(b + 8, b % 2)
                    y_high(0)
                    y_high(1)
                    u_gelu(3)
                    y_high(2)
                    y_high(3)
                    split(b + 9, (b + 9) % 2)
                    for g in range(4, G):
                        y_high(g)
                    split(b + 10, b % 2)
                    split(b + 11, (b + 11) % 2)
                    split(b + 12, b % 2)
                if kind == "attn":
                    def v_out(c):
                        act.wait_ge(w_used, 2 * b + (6 if c == 0 else 12))
                        act.wait_ge(rstd_ready, s + 1)
                        for tt in range(TT):
                            act.activation(vt[:, tt, c * T:(c + 1) * T], bank[4 + tt][:, :], ACT.Copy,
                                           scale=rstd[:, tt:tt + 1]).then_inc(v_ready, 1)

                    def qk_high(p, par, c):
                        act.wait_ge(qy_ready, 2 * p + c + 1)
                        act.activation(qk_hi[:, par, c, :], qy[:, c, :], ACT.Copy,
                                       scale=QSCALE if c == 0 else 1.0).then_inc(qk_hi_ready, 1)

                    def keep_exp(n, e):
                        act.wait_ge(z_ready, n + 1)
                        if not (isinstance(n, int) and n < 2):
                            act.wait_ge(alo_ready, n - 1)
                        for p0, p1, s0, s1 in PIECES:
                            act.activation(e_t[:, e, s0:s1], psum[:, Z0[e] + p0:Z0[e] + p1], ACT.Abs).then_inc(e_step, 1)
                        act.wait_ge(e_step, 4 * n + 2)
                        act.activation(e_t[:, e, :], e_t[:, e, :], ACT.Exp, scale=-1.0).then_inc(e_step, 1)

                    def keep_ln(n, e):
                        act.wait_ge(e_step, 4 * n + 3)
                        act.activation(e_t[:, e, :], e_t[:, e, :], ACT.Ln, bias=ones[:, 0:1]).then_inc(e_step, 1)

                    def weights(n, e):
                        act.wait_ge(loga_ready, n + 1)
                        for p0, p1, s0, s1 in PIECES:
                            act.activation(e_t[:, e, s0:s1], psum[:, Z0[e] + p0:Z0[e] + p1], ACT.Exp).then_inc(a_ready, 1)

                    def head_out(n, p, e):
                        act.wait_ge(o_ready, n + 1)
                        rows = slice(HD * e, HD * e + HD)
                        act.activation(o_hi[rows, bass.ds(p, 1), :], bank[6][rows, :].rearrange("p (a n) -> p a n", a=1),
                                       ACT.Copy).then_inc(ohi_ready, 1)

                    def head_pair(p, par, more, last=False):
                        for e in range(2):
                            n = 2 * p + e
                            if not (last and e):
                                keep_exp(n + 1, 1 - e)
                            weights(n, e)
                            if not (last and e):
                                keep_ln(n + 1, 1 - e)
                            if more:
                                split_unit(p + (b + 8), (b + par) % 2, e)
                                qk_high(p + 2, par, e)
                            head_out(n, p, e)

                    qk_high(0, 0, 0)
                    qk_high(0, 0, 1)
                    split(b + 3, (b + 3) % 2)
                    v_out(0)
                    split(b + 4, b % 2)
                    qk_high(1, 1, 0)
                    qk_high(1, 1, 1)
                    split(b + 5, (b + 5) % 2)
                    act.preload_act_table_set("natural_log_exp_and_others")
                    keep_exp(0, 0)
                    keep_ln(0, 0)
                    split(b + 6, b % 2)
                    v_out(1)
                    split(b + 7, (b + 7) % 2)
                    head_pair(0, 0, True)
                    head_pair(1, 1, True)
                    with act.Fori(1, 3) as i:
                        head_pair(2 * i, 0, True)
                        head_pair(2 * i + 1, 1, True)
                    head_pair(6, 0, False)
                    head_pair(7, 1, False, last=True)
                    def squares(d):
                        for half in (A, B):
                            out_square(s, d, half)

                    split(b + 14, b % 2)
                    squares(0)
                    squares(1)
                    split(b + 15, (b + 15) % 2)
                    for d in range(2, 5):
                        squares(d)
                    split_unit(b + 16, b % 2, 0)
                    squares(5)
                    split_unit(b + 16, b % 2, 1)
                post(s)
            boundary(NSUB)
            for q in (0, 1, 2, 3, 5, 7):
                act.wait_ge(out_turned, q + 1)
                act.activation(o_tok[:, q // 2, (q % 2) * T:(q % 2 + 1) * T], bank[TURN[q]][:, :],
                               ACT.Copy).then_inc(out_by_act, 1)

        @block.vector
        def _(dve):
            def split_unit(pair, par, c):
                dve.wait_ge(hi_ready, 2 * pair + c + 1)
                dve.tensor_tensor(w_lo[:, 2 * par + c, :], raw[:, c, :], w_hi[:, 2 * par + c, :].bitcast(F32),
                                  ALU.subtract).then_inc(lo_ready, 1)

            def split(pair, par):
                split_unit(pair, par, 0)
                split_unit(pair, par, 1)

            def pre_lo(s, d, half):
                hs = HALF[half]
                dve.wait_ge(xhi_ready[half], 8 * s + d + 1)
                dve.scalar_tensor_tensor(out=xn_lo[:, d, hs], in0=h[:, d, hs], scalar=gain(True, s, d),
                                         in1=xn_hi[:, d, hs].bitcast(F32), op0=ALU.mult,
                                         op1=ALU.subtract).then_inc(xlo_ready[half], 1)

            def diagonals(inv, tiles):
                for tt in tiles:
                    last = dve.tensor_scalar(diag[:, tt, :], ident[:, :], inv[:, tt:tt + 1], None, ALU.mult)
                return last

            def pre_norm(s):
                dve.wait_ge(hsq_ready, 8 * s + 4)
                dve.tensor_tensor(sqb[:, :], m[:, 1, :], m[:, 3, :], ALU.add).then_inc(hsum_odd, 1)
                for i, d in enumerate((5, 7)):
                    dve.wait_ge(hsq_ready, 8 * s + d + 1)
                    dve.wait_ge(hsum_odd, 3 * s + i + 1)
                    dve.tensor_tensor(sqb[:, :], sqb[:, :], m[:, d, :], ALU.add).then_inc(hsum_odd, 1)
                b = BASE[s]
                split(b + 2, b % 2)
                dve.wait_ge(std_ready, s + 1)
                dve.reciprocal(rstd[:, :], std[:, :]).then_inc(rstd_ready, 1)
                dve.wait_ge(rstd_ready, s + 1)
                diagonals(rstd, range(TT)).then_inc(hdiag_ready, 1)
                if SUBS[s][0] == "ffn":
                    dve.scalar_tensor_tensor(out=e2[:, :], in0=std[:, :], scalar=RMS_EPS, in1=std[:, :],
                                             op0=ALU.mult, op1=ALU.mult).then_inc(e2_ready, 1)
                dve.wait_ge(hbc_ready, s + 1)
                dve.tensor_copy(rbc[:, :], bank[3][:, :]).then_inc(rbc_ready, 1)

            def out_evac(s, d, half):
                hs = HALF[half]
                wait_out(dve, s, d, half)
                if SUBS[s][0] == "attn" and d < EARLY:
                    dve.wait_ge(part_ready, EARLY)
                    dve.tensor_tensor(m[:, d, hs], bank[d][:, hs], part[:, d, hs], ALU.add).then_inc(m_evac[half], 1)
                else:
                    dve.tensor_copy(m[:, d, hs], bank[d][:, hs]).then_inc(m_evac[half], 1)

            def post(s):
                for d in range(KC - 2 if SUBS[s][0] == "attn" else 0, KC):
                    out_evac(s, d, A)

            def out_mean(s, half):
                if SUBS[s][0] == "ffn":
                    cols = COLS[half]
                    dve.wait_ge(mtotal_ready[half], s + 1)
                    dve.wait_ge(e2_ready, ffn_index(s) + 1)
                    dve.scalar_tensor_tensor(out=m_mean[:, cols], in0=bank[2][:, cols], scalar=1.0 / DM, in1=e2[:, cols],
                                             op0=ALU.mult, op1=ALU.add).then_inc(mmean_ready[half], 1)

            def out_inverse(s, half):
                dve.wait_ge(mroot_ready[half], s + 1)
                dve.reciprocal(m_inv[:, COLS[half]], m_root[:, COLS[half]]).then_inc(minv_ready[half], 1)
                dve.wait_ge(minv_ready[half], s + 1)
                diagonals(m_inv, (2 * half, 2 * half + 1)).then_inc(mdiag_ready[half], 1)

            def step(s, d, half):
                hs = HALF[half]
                dve.scalar_tensor_tensor(out=m[:, d, hs], in0=m[:, d, hs], scalar=gain(False, s, d),
                                         in1=bank[RBANK[half]][:, hs], op0=ALU.mult,
                                         op1=ALU.mult).then_inc(applied[half], 1)
                if d < own_adds(s):
                    dve.wait_ge(applied[half], 8 * s + d + 1)
                    dve.tensor_tensor(h[:, d, hs], h[:, d, hs], m[:, d, hs], ALU.add).then_inc(h_ready[half], 1)

            def boundary(s):
                last = s == NSUB
                t = s - 1

                def lo(d, half):
                    if not last:
                        pre_lo(s, d, half)

                out_mean(t, A)
                out_inverse(t, A)
                dve.wait_ge(mbc_ready[A], t + 1)
                for name in ORDER[:-1]:
                    d = int(name[1])
                    if name[0] == "L":
                        lo(d, A)
                    else:
                        step(t, d, A)
                        if d == KC - 2:
                            out_mean(t, B)
                        if d == KC - 1:
                            out_inverse(t, B)
                dve.wait_ge(mbc_ready[B], t + 1)
                for name in ORDER[:-2]:
                    d = int(name[1])
                    if name[0] == "L":
                        lo(d, B)
                    else:
                        step(t, d, B)
                        if d == 0:
                            lo(KC - 1, A)
                if last:
                    return
                b = BASE[s]
                split_unit(b + 1, (b + 1) % 2, 0)
                lo(KC - 2, B)
                lo(KC - 1, B)
                split_unit(b + 1, (b + 1) % 2, 1)

            def start():
                for j in range(KC // 2):
                    dve.wait_ge(x_turned[A], j + 1)
                    dve.tensor_copy(h[:, 2 * j:2 * j + 2, HALF[A]],
                                    bank[XBANK[A][j]][:, :].rearrange("p (c t) -> p c t", c=2)).then_inc(h_ready[A], 2)
                dve.wait_ge(gains_ready, 1)
                for d in range(4):
                    pre_lo(0, d, A)
                split(0, 0)
                for d in range(4, KC):
                    pre_lo(0, d, A)
                for d in range(KC):
                    pre_lo(0, d, B)
                split(1, 1)

            dve.wait_ge(const_ready, 10)
            dve.tensor_copy(neg_tri[:, :], tri_f[:, 0, :]).then_inc(const2_ready, 1)
            dve.tensor_copy(neg_ones[:, :], tri_f[:, 1, :]).then_inc(const2_ready, 1)
            dve.tensor_copy(mask_bf[:, :], tri_f[:, 2:4, :].rearrange("p a n -> p (a n)")).then_inc(const2_ready, 1)
            dve.tensor_copy(ident_bf[:, :], ident[:, :]).then_inc(const2_ready, 1)
            dve.wait_ge(gains_turned, 1)
            dve.tensor_copy(gcol[:, 0:NG], bank[3][:, 0:NG]).then_inc(gains_ready, 1)

            for s, (kind, _, _) in enumerate(SUBS):
                b = BASE[s]
                if s:
                    boundary(s)
                else:
                    start()
                pre_norm(s)
                dve.wait_ge(rbc_ready, s + 1)
                if kind == "ffn":
                    q0 = NF * ffn_index(s)

                    def hidden(f, c, pair):
                        dve.wait_ge(w_used, 2 * f + (2 * b + 2))
                        dve.tensor_tensor(t1[:, c, :], bank[HB[c]][:, :], rbc[:, :], ALU.mult).then_inc(t1_ready, 1)
                        if pair is not None:
                            split_unit(pair, (b + c) % 2, 0)
                        dve.wait_ge(silu_ready, q0 + f + 1)
                        dve.tensor_tensor(yf[:, c, :], bank[HB[c] + 1][:, :], t1[:, c, :], ALU.mult).then_inc(y_ready, 1)
                        if pair is not None:
                            split_unit(pair, (b + c) % 2, 1)
                        dve.wait_ge(hid_hi_ready, q0 + f + 1)
                        dve.tensor_tensor(hid_lo[:, bass.ds(f, 1), :], yf[:, c:c + 1, :],
                                          hid_hi[:, bass.ds(f, 1), :].bitcast(F32), ALU.subtract).then_inc(hid_lo_ready, 1)

                    hidden(0, 0, None)
                    hidden(1, 1, b + 3)
                    with dve.Fori(1, NF // 2) as i:
                        for c in range(2):
                            hidden(2 * i + c, c, 2 * i + (b + c + 2))
                    last = s == NSUB - 1
                    with dve.Fori(0, 4 if last else 5) as i:
                        for c in range(2):
                            split(2 * i + (b + NF + c + 2), (b + c) % 2)
                    if last:
                        split(b + NF + 10, b % 2)
                if kind == "gmlp":
                    def u_scale(i):
                        pair = b + (0, 3, 6, 7)[i]
                        dve.wait_ge(w_used, 2 * pair + 2)
                        for c in range(2):
                            if i:
                                dve.wait_ge(u_ready, 2 * i + c - 1)
                            dve.tensor_tensor(ut[:, c, :], bank[2 * (i % 2) + c][:, :], rbc[:, :],
                                              ALU.mult).then_inc(ut_ready, 1)

                    def gate(g):
                        dve.wait_ge(sp_done, g + 1)
                        dve.wait_ge(gm_loaded, 32)
                        if g >= 4:
                            dve.wait_ge(ylo_ready, g - 3)
                        dve.scalar_tensor_tensor(
                            out=yt[:, g % 4, :].rearrange("p (c t) -> p c t", c=TT),
                            in0=bank[4 + g % 4][:, :].rearrange("p (c t) -> p c t", c=TT),
                            scalar=gcol[:, 12 * KC + g:12 * KC + g + 1],
                            in1=bias_bc[:, g:g + 1, :].broadcast_to([P, TT, P]),
                            op0=ALU.mult, op1=ALU.add).then_inc(yt_ready, 1)

                    def gated(g):
                        dve.wait_ge(yt_ready, g + 1)
                        dve.wait_ge(u_ready, g + 1)
                        dve.tensor_tensor(yt[:, g % 4, :], yt[:, g % 4, :], u[:, g, :], ALU.mult).then_inc(ym_ready, 1)

                    def y_low(g):
                        dve.wait_ge(yhi_ready, g + 1)
                        dve.tensor_tensor(y_lo[:, g, :], yt[:, g % 4, :], y_hi[:, g, :].bitcast(F32),
                                          ALU.subtract).then_inc(ylo_ready, 1)

                    u_scale(0)
                    split(b + 3, (b + 3) % 2)
                    split(b + 4, b % 2)
                    u_scale(1)
                    split(b + 5, (b + 5) % 2)
                    split(b + 6, b % 2)
                    dve.wait_ge(v_ready, 2 * TT)
                    dve.tensor_tensor(vst[:, 8:12], vst[:, 0:4], vst[:, 4:8], ALU.add).then_inc(ln_step, 1)
                    dve.wait_ge(ln_step, 1)
                    dve.tensor_scalar(vst[:, 12:16], vst[:, 8:12], -1.0 / DM, None, ALU.mult).then_inc(ln_step, 1)
                    split(b + 7, (b + 7) % 2)
                    dve.wait_ge(ln_std, 1)
                    dve.reciprocal(vst[:, 24:28], vst[:, 20:24]).then_inc(ln_step, 1)
                    dve.wait_ge(ln_step, 3)
                    for tt in range(TT):
                        dve.tensor_scalar(v[:, tt, :], v[:, tt, :], vst[:, 12 + tt:13 + tt], vst[:, 24 + tt:25 + tt],
                                          ALU.add, ALU.mult).then_inc(vn_ready, 1)
                    u_scale(2)
                    split(b + 8, b % 2)
                    gate(0)
                    gate(1)
                    for g in range(2):
                        gated(g)
                    for g in range(2):
                        y_low(g)
                    u_scale(3)
                    for g in range(2, 6):
                        gate(g)
                    gated(2)
                    gated(3)
                    for g in range(2, G):
                        y_low(g)
                        if g + 4 < G:
                            gate(g + 4)
                        if g + 2 < G:
                            gated(g + 2)
                        if g == 3:
                            split(b + 9, (b + 9) % 2)
                    split(b + 10, b % 2)
                    split(b + 11, (b + 11) % 2)
                    split(b + 12, b % 2)
                if kind == "attn":
                    def qk_out(c, src):
                        dve.tensor_tensor(qy[:, c, :], src[:, :], rbc[:, :], ALU.mult).then_inc(qy_ready, 1)

                    def qk_low(p, par, c):
                        dve.wait_ge(qk_hi_ready, 2 * p + c + 1)
                        dve.scalar_tensor_tensor(
                            out=qk_lo[:, par, c, :], in0=qy[:, c, :], scalar=QSCALE if c == 0 else 1.0,
                            in1=qk_hi[:, par, c, :].bitcast(F32), op0=ALU.mult, op1=ALU.subtract).then_inc(qk_lo_ready, 1)

                    def keep(n, e, between=None):
                        dve.wait_ge(e_step, 4 * n + 4)
                        for p0, p1, s0, s1 in PIECES:
                            dve.scalar_tensor_tensor(out=e_t[:, e, s0:s1], in0=psum[:, Z0[e] + p0:Z0[e] + p1], scalar=0.0,
                                                     in1=e_t[:, e, s0:s1], op0=ALU.max, op1=ALU.add).then_inc(sp_ready, 1)
                        dve.wait_ge(sp_ready, 2 * n + 2)
                        if not (isinstance(n, int) and n < 2):
                            dve.wait_ge(o_ready, n - 1)
                        dve.tensor_copy(p_hi[:, e, :], e_t[:, e, :]).then_inc(sphi_ready, 1)
                        if between:
                            between()
                        dve.wait_ge(sphi_ready, n + 1)
                        dve.tensor_tensor(p_lo[:, e, :], e_t[:, e, :], p_hi[:, e, :].bitcast(F32),
                                          ALU.subtract).then_inc(splo_ready, 1)

                    def weights(n, e):
                        dve.wait_ge(a_ready, 2 * n + 2)
                        dve.tensor_copy(p_hi[:, e, :], e_t[:, e, :]).then_inc(ahi_ready, 1)
                        dve.wait_ge(ahi_ready, n + 1)
                        dve.tensor_tensor(p_lo[:, e, :], e_t[:, e, :], p_hi[:, e, :].bitcast(F32),
                                          ALU.subtract).then_inc(alo_ready, 1)

                    def head_out(n, p, e):
                        dve.wait_ge(ohi_ready, n + 1)
                        rows = slice(HD * e, HD * e + HD)
                        dve.tensor_tensor(o_lo[rows, bass.ds(p, 1), :], bank[6][rows, :].rearrange("p (a n) -> p a n", a=1),
                                          o_hi[rows, bass.ds(p, 1), :].bitcast(F32), ALU.subtract).then_inc(olo_ready, 1)

                    def head_pair(p, par, more, last=False):
                        for e in range(2):
                            n = 2 * p + e
                            weights(n, e)

                            def project_out():
                                if more:
                                    dve.wait_ge(w_used, 2 * p + (2 * b + 13 + e))
                                    qk_out(e, bank[7])
                                else:
                                    d = n - (2 * HEAD_PAIRS - EARLY)
                                    dve.wait_ge(part_done, d + 1)
                                    dve.tensor_copy(part[:, d, :], bank[7][:, :]).then_inc(part_ready, 1)

                            if last and e:
                                project_out()
                            else:
                                keep(n + 1, 1 - e, project_out)
                            if more:
                                qk_low(p + 2, par, e)
                            head_out(n, p, e)

                    for c in range(2):
                        qk_out(c, bank[c])
                        qk_low(0, 0, c)
                    split(b + 3, (b + 3) % 2)
                    split(b + 4, b % 2)
                    dve.wait_ge(w_used, 2 * b + 8)
                    for c in range(2):
                        qk_out(c, bank[2 + c])
                        qk_low(1, 1, c)
                    split(b + 5, (b + 5) % 2)
                    keep(0, 0)
                    split(b + 6, b % 2)
                    split(b + 7, (b + 7) % 2)
                    head_pair(0, 0, True)
                    head_pair(1, 1, True)
                    with dve.Fori(1, 3) as i:
                        head_pair(2 * i, 0, True)
                        head_pair(2 * i + 1, 1, True)
                    head_pair(6, 0, False)
                    head_pair(7, 1, False, last=True)
                    dve.wait_ge(lo_ready, 2 * b + 28)
                    def evac(d):
                        for half in (A, B):
                            out_evac(s, d, half)

                    split(b + 14, b % 2)
                    evac(0)
                    evac(1)
                    split(b + 15, (b + 15) % 2)
                    for d in range(2, 5):
                        evac(d)
                    split_unit(b + 16, b % 2, 0)
                    evac(5)
                    split_unit(b + 16, b % 2, 1)
                post(s)
            boundary(NSUB)
            for q in (4, 6):
                dve.wait_ge(out_turned, q + 1)
                dve.tensor_copy(o_tok[:, q // 2, 0:T], bank[TURN[q]][:, :]).then_inc(out_by_dve, 1)

        @block.tensor
        def _(pe):
            def passes(dst, a_hi, a_lo, b_hi, b_lo, start, stop, onto=False):
                pe.matmul(dst, a_hi, b_hi, start=start, stop=False, skip_group_check=onto)
                pe.matmul(dst, a_hi, b_lo, start=False, stop=False, skip_group_check=onto)
                return pe.matmul(dst, a_lo, b_hi, start=False, stop=stop, skip_group_check=onto)

            def split_ready(pair):
                pe.wait_ge(lo_ready, 2 * pair + 2)

            def totals(dst, squares, tiles, waits=None):
                for i, x2 in enumerate(squares):
                    if waits and i:
                        waits(i)
                    for tt in tiles:
                        last = pe.matmul(dst[:, tt:tt + 1], x2[:, tt * P:(tt + 1) * P], ones[:, 0:1],
                                         start=i == 0 and tt == tiles[0], stop=i == len(squares) - 1,
                                         skip_group_check=True)
                return last

            def pre_total(s):
                pe.wait_ge(hsum_even, 3 * s + 3)
                pe.wait_ge(hsum_odd, 3 * s + 3)
                totals(bank[2], [sqa, sqb], range(TT)).then_inc(htotal_ready, 1)

            def pre_broadcast(s):
                pe.wait_ge(hdiag_ready, s + 1)
                pe.matmul(bank[3][:, :], ones[:, :], diag[:, :, :].rearrange("p c t -> p (c t)"), start=True,
                          stop=True).then_inc(hbc_ready, 1)

            def out_total(s, half):
                pe.wait_ge(msum_ready[half], (SUMMED[half] - 1) * (s + 1))
                if half == A:
                    pe.wait_ge(msq_ready[B], 8 * s + 3)
                else:
                    pe.wait_ge(mroot_ready[A], s + 1)
                rest = [sq[:, d, :] for d in range(SUMMED[half], KC)]
                totals(bank[2], [sqa] + rest, (2 * half, 2 * half + 1),
                       lambda i: pe.wait_ge(msq_ready[half], 8 * s + SUMMED[half] + i)).then_inc(mtotal_ready[half], 1)

            def out_broadcast(s, half):
                pe.wait_ge(mdiag_ready[half], s + 1)
                pe.wait_ge(msq_ready[B], 8 * s + RBANK[half] + 1)
                pe.matmul(bank[RBANK[half]][:, HALF[half]], ones[:, :],
                          diag[:, 2 * half:2 * half + 2, :].rearrange("p c t -> p (c t)"), start=True, stop=True,
                          skip_group_check=True).then_inc(mbc_ready[half], 1)

            def first_pair(s, pair, at):
                par = pair % 2
                split_ready(pair)
                for half in (A, B):
                    hs = HALF[half]
                    for k in range(KC):
                        w = slice(k * P, (k + 1) * P)
                        pe.wait_ge(xhi_ready[half], 8 * s + k + 1)
                        for c in range(2):
                            pe.matmul(bank[at + c][:, hs], w_hi[:, 2 * par + c, w], xn_hi[:, k, hs], start=k == 0,
                                      stop=False, skip_group_check=True)
                            pe.matmul(bank[at + c][:, hs], w_lo[:, 2 * par + c, w], xn_hi[:, k, hs], start=False,
                                      stop=False, skip_group_check=True)
                        pe.wait_ge(xlo_ready[half], 8 * s + k + 1)
                        for c in range(2):
                            last = pe.matmul(bank[at + c][:, hs], w_hi[:, 2 * par + c, w], xn_lo[:, k, hs], start=False,
                                             stop=k == KC - 1, skip_group_check=True)
                        if half == A and k == 1 and s:
                            out_total(s - 1, B)
                        if half == A and k == 4 and s:
                            out_broadcast(s - 1, B)
                last.then_inc(w_used, 2)

            def columns_pair(par, pair, at):
                split_ready(pair)
                for k in range(KC):
                    w = slice(k * P, (k + 1) * P)
                    for c in range(2):
                        last = passes(bank[at + c][:, :], w_hi[:, 2 * par + c, w], w_lo[:, 2 * par + c, w],
                                      xn_hi[:, k, :], xn_lo[:, k, :], k == 0, k == KC - 1)
                last.then_inc(w_used, 2)

            def column_unit(par, c, dst, after=None):
                for k in range(KC):
                    w = slice(k * P, (k + 1) * P)
                    last = passes(dst[:, :], w_hi[:, 2 * par + c, w], w_lo[:, 2 * par + c, w],
                                  xn_hi[:, k, :], xn_lo[:, k, :], k == 0, k == KC - 1)
                    if after and k < KC - 1:
                        after(k)
                last.then_inc(w_used, 1)

            def tokens_unit(pair, half, c):
                par = pair % 2
                pe.wait_ge(lo_ready, 2 * pair + c + 1)
                for kk in range(2):
                    k = 4 * half + 2 * c + kk
                    for tt in range(TT):
                        tk = slice(tt * P, (tt + 1) * P)
                        w = slice(kk * T, (kk + 1) * T)
                        last = passes(bank[4 + tt][:, :], xn_hi[:, k, tk], xn_lo[:, k, tk],
                                      w_hi[:, 2 * par + c, w], w_lo[:, 2 * par + c, w], k == 0, k == KC - 1)
                last.then_inc(w_used, 1)

            def tokens_pair(pair, half):
                for c in range(2):
                    tokens_unit(pair, half, c)

            def project_unit(par, c, x_hi, x_lo, start, bank_wait=None):
                for d in range(KC):
                    if bank_wait:
                        bank_wait(d)
                    w = slice(d * P, (d + 1) * P)
                    last = passes(bank[d][:, :], w_hi[:, 2 * par + c, w], w_lo[:, 2 * par + c, w], x_hi, x_lo,
                                  start, True, onto=not start)
                last.then_inc(w_used, 1)

            def output_half(dst, half, units, after=None):
                hs = HALF[half]
                for i, (a_hi, a_lo, x_hi, x_lo, start) in enumerate(units):
                    stop = i == len(units) - 1
                    pe.matmul(dst[:, hs], a_hi, x_hi[:, hs], start=start, stop=False, skip_group_check=True)
                    pe.matmul(dst[:, hs], a_hi, x_lo[:, hs], start=False, stop=False, skip_group_check=True)
                    last = pe.matmul(dst[:, hs], a_lo, x_hi[:, hs], start=False, stop=stop, skip_group_check=True)
                    if after and not stop:
                        after(i)
                return last

            def project_last(s, par, x_hi, x_lo):
                for half in (A, B):
                    for d in range(KC):
                        w = slice(d * P, (d + 1) * P)
                        if half == B:
                            pe.wait_ge(m_evac[A], 8 * s + d + 1)
                        last = output_half(bank[d], half, [
                            (w_hi[:, 2 * par + c, w], w_lo[:, 2 * par + c, w], x_hi[:, c, :], x_lo[:, c, :], False)
                            for c in range(2)])
                        if half == A or d < KC - 1:
                            last.then_inc(acc_done[half], 1)
                        else:
                            last.then_inc(w_used, 2)
                        if half == B and d == 3:
                            out_total(s, A)
                        if half == B and d == 5:
                            out_broadcast(s, A)

            def mixer_start(s, b, v_count):
                first_pair(s, b, 0)
                tokens_unit(b + 1, 0, 0)
                pre_total(s)
                tokens_unit(b + 1, 0, 1)
                pre_broadcast(s)
                tokens_pair(b + 2, 1)
                pe.wait_ge(rbc_ready, s + 1)
                columns_pair((b + 3) % 2, b + 3, 2)
                pe.wait_ge(v_ready, v_count)
                tokens_pair(b + 4, 0)

            pe.wait_ge(const_ready, 10)
            pe.wait_ge(g_loaded, 48)
            pe.transpose(bank[3][:, 0:NG], g_rows[0:NG, :], ident[0:NG, 0:NG]).then_inc(gains_turned, 1)
            for half in (A, B):
                pe.wait_ge(x_loaded[half], 32)
                for j in range(KC // 2):
                    if half == B and j == 1:
                        pe.wait_ge(gains_ready, 1)
                    if half == B and j >= 2:
                        pe.wait_ge(h_ready[A], 2 * j - 2)
                    for d in (2 * j, 2 * j + 1):
                        for tt in (2 * half, 2 * half + 1):
                            at = (d % 2) * (T // 2) + (tt % 2) * P
                            last = pe.transpose(bank[XBANK[half][j]][:, at:at + P], x_in[:, tt, d * P:(d + 1) * P],
                                                ident[:, :])
                    last.then_inc(x_turned[half], 1)

            for s, (kind, _, _) in enumerate(SUBS):
                b = BASE[s]
                if kind == "ffn":
                    q0 = NF * ffn_index(s)
                    first_pair(s, b, HB[0])
                    for c in range(2):
                        pe.wait_ge(lo_ready, 2 * (b + 1) + c + 1)
                        column_unit((b + 1) % 2, c, bank[HB[1] + c],
                                    lambda k: pre_broadcast(s) if c == 1 and k == 2 else None)
                        if c == 0:
                            pre_total(s)
                    with pe.Fori(1, NF // 2) as i:
                        for c in range(2):
                            pe.wait_ge(y_ready, 2 * i + (q0 + c - 1))
                            columns_pair((b + c) % 2, 2 * i + (b + c), HB[c])

                    def hidden_free(d):
                        if d in HB:
                            pe.wait_ge(y_ready, q0 + NF - 1 + (d == HB[1]))

                    for f in range(4):
                        if f % 2 == 0:
                            split_ready(b + NF + f // 2)
                        pe.wait_ge(hid_lo_ready, q0 + f + 1)
                        project_unit((b + f // 2) % 2, f % 2, hid_hi[:, f, :], hid_lo[:, f, :], f == 0,
                                     hidden_free if f == 0 else None)
                    with pe.Fori(1, 5) as i:
                        for c in range(2):
                            split_ready(2 * i + (b + NF + c))
                            for e in range(2):
                                pe.wait_ge(hid_lo_ready, 4 * i + (q0 + 2 * c + e + 1))
                                project_unit((b + c) % 2, e, hid_hi[:, bass.ds(4 * i + (2 * c + e), 1), :],
                                             hid_lo[:, bass.ds(4 * i + (2 * c + e), 1), :], False)
                    pe.wait_ge(hid_lo_ready, q0 + NF)
                    split_ready(b + NF + NF // 2 - 1)
                    project_last(s, (b + NF // 2 - 1) % 2, hid_hi[:, NF - 2:NF, :], hid_lo[:, NF - 2:NF, :])
                if kind == "gmlp":
                    mixer_start(s, b, TT)
                    tokens_pair(b + 5, 1)
                    pe.wait_ge(ut_ready, 2)
                    columns_pair(b % 2, b + 6, 0)
                    pe.wait_ge(v_ready, 2 * TT)
                    pe.wait_ge(ws_masked, 1)
                    for g in range(G):
                        last = pe.transpose(bank[4 + g // 4][:, (g % 4) * P:(g % 4 + 1) * P], ws_raw[:, g, :], ident[:, :])
                    last.then_inc(ws_turned, 1)

                    def mix(g):
                        if g >= 4:
                            pe.wait_ge(yt_ready, g - 3)
                        for c in range(TT):
                            last = pe.matmul(bank[4 + g % 4][:, c * P:(c + 1) * P], v[:, c, g * P:(g + 1) * P],
                                             wsT[:, g, :], start=True, stop=True)
                        last.then_inc(sp_done, 1)

                    pe.wait_ge(ut_ready, 4)
                    split_ready(b + 7)
                    column_unit((b + 7) % 2, 0, bank[2])
                    pe.wait_ge(ws_ready, 2)
                    pe.wait_ge(vn_ready, TT)
                    mix(0)
                    mix(1)
                    column_unit((b + 7) % 2, 1, bank[3])
                    for g in range(2, G):
                        mix(g)
                    pe.wait_ge(ut_ready, 8)

                    def mixed_free(d):
                        if d >= 4:
                            pe.wait_ge(yt_ready, d + 1)

                    for k in range(6):
                        if k % 2 == 0:
                            split_ready(b + 8 + k // 2)
                        pe.wait_ge(ylo_ready, k + 1)
                        project_unit((b + k // 2) % 2, k % 2, y_hi[:, k, :], y_lo[:, k, :], k == 0,
                                     mixed_free if k == 0 else None)
                    split_ready(b + 11)
                    pe.wait_ge(ylo_ready, KC)
                    project_last(s, (b + 11) % 2, y_hi[:, 6:8, :], y_lo[:, 6:8, :])
                if kind == "attn":
                    mixer_start(s, b, 3 * TT)

                    def scores(n, e, par):
                        if not (isinstance(n, int) and n < 2):
                            pe.wait_ge(a_ready, 2 * n - 2)
                        rows = slice(HD * e, HD * e + HD)
                        for i in range(TT):
                            keys = slice(P * i, P * i + P)
                            q = slice(BQ[i], T)
                            at, col = BPOS[i]
                            dst = bank[3 * e + at][:, col:col + T - BQ[i]]
                            k_hi, k_lo = qk_hi[rows, par, 1, keys], qk_lo[rows, par, 1, keys]
                            q_hi, q_lo = qk_hi[rows, par, 0, q], qk_lo[rows, par, 0, q]
                            pe.matmul(dst, k_hi, q_hi, start=i < 3, stop=False, skip_group_check=i == 3)
                            pe.matmul(dst[:, 0:P * (1 + (i == 3))], ident_bf[:, :], mask_bf[:, P * (i < 3):2 * P],
                                      start=False, stop=False, skip_group_check=True)
                            pe.matmul(dst, k_hi, q_lo, start=False, stop=False, skip_group_check=i == 3)
                            last = pe.matmul(dst, k_lo, q_hi, start=False, stop=True, skip_group_check=i == 3)
                        last.then_inc(z_ready, 1)

                    def log_weights(n, e):
                        pe.wait_ge(splo_ready, n + 1)
                        for i in range(TT):
                            at, col = BPOS[i]
                            for c in range(i, TT):
                                dst = bank[3 * e + at][:, col + BQ[c] - BQ[i]:col + T - BQ[i]]
                                lhs = neg_tri if c == i else neg_ones
                                for part in (p_hi, p_lo):
                                    last = pe.matmul(dst, lhs[:, :], part[:, e, BOFF[c]:BOFF[c] + T - BQ[c]], start=False,
                                                     stop=True, skip_group_check=True)
                        last.then_inc(loga_ready, 1)

                    def weighted(n, p, e):
                        pe.wait_ge(alo_ready, n + 1)
                        pe.wait_ge(vp_ready, 2 * p + 2)
                        if not (isinstance(n, int) and n == 0):
                            pe.wait_ge(olo_ready, n)
                        for i in range(TT):
                            cols = slice(BOFF[i], BOFF[i] + T - BQ[i])
                            last = passes(bank[6][:, BQ[i]:T], vp_hi[:, i, :], vp_lo[:, i, :],
                                          p_hi[:, e, cols], p_lo[:, e, cols], i == 0, i == TT - 1)
                        last.then_inc(o_ready, 1)

                    def from_heads(par, c, dst, k, start, stop):
                        w = slice(k * P, (k + 1) * P)
                        return passes(dst[:, :], w_hi[:, 2 * par + c, w], w_lo[:, 2 * par + c, w],
                                      o_hi[:, k, :], o_lo[:, k, :], start, stop)

                    def done_pairs(d):
                        return (2 * HEAD_PAIRS - EARLY + d) // 2

                    def early_output(n, par, c):
                        d = n - (2 * HEAD_PAIRS - EARLY)
                        split_ready(b + 12 + d // 2)
                        pe.wait_ge(olo_ready, 2 * done_pairs(d))
                        if d == 0:
                            pe.wait_ge(qy_ready, 2 * HEAD_PAIRS)
                        else:
                            pe.wait_ge(part_ready, d)
                        for k in range(done_pairs(d)):
                            last = from_heads((b + par) % 2, c, bank[7], k, k == 0, k == done_pairs(d) - 1)
                        last.then_inc(part_done, 1)

                    def head_pair(p, par, more, last=False):
                        for e in range(2):
                            n = 2 * p + e
                            first = isinstance(n, int) and n == 0
                            if first:
                                log_weights(0, 0)
                                pe.wait_ge(v_ready, 4 * TT)
                            if not (last and e):
                                if e:
                                    pe.wait_ge(qk_lo_ready, 2 * p + 4)
                                scores(n + 1, 1 - e, par if e == 0 else 1 - par)
                            if not first:
                                log_weights(n, e)
                            if more:
                                if e == 0:
                                    split_ready(p + (b + 6))
                                pe.wait_ge(qy_ready, 2 * p + 4 + e)
                                column_unit((b + par) % 2, e, bank[7])
                            else:
                                early_output(n, par, e)
                            weighted(n, p, e)

                    pe.wait_ge(const2_ready, 4)
                    pe.wait_ge(qk_lo_ready, 2)
                    pe.wait_ge(qy_ready, 4)
                    scores(0, 0, 0)
                    tokens_pair(b + 5, 1)
                    head_pair(0, 0, True)
                    head_pair(1, 1, True)
                    with pe.Fori(1, 3) as i:
                        head_pair(2 * i, 0, True)
                        head_pair(2 * i + 1, 1, True)
                    head_pair(6, 0, False)
                    head_pair(7, 1, False, last=True)
                    for d in range(2):
                        from_heads(b % 2, d, bank[d], 6, True, False)
                    pe.wait_ge(olo_ready, 2 * HEAD_PAIRS)
                    for d in range(EARLY):
                        from_heads((b + d // 2) % 2, d % 2, bank[d], 7, d >= 2, True).then_inc(w_used, 1)
                    pe.wait_ge(part_ready, EARLY)
                    for d in range(EARLY, KC - 2):
                        pe.wait_ge(lo_ready, 2 * (b + 12) + d + 1)
                        for k in range(KC):
                            last = from_heads((b + d // 2) % 2, d % 2, bank[d], k, k == 0, k == KC - 1)
                        last.then_inc(w_used, 1)
                    def norm_a(s, d, i):
                        if (d, i) == (KC - 2, 4):
                            out_total(s, A)
                        if (d, i) == (KC - 1, 2):
                            out_broadcast(s, A)

                    for half in (A, B):
                        for d in (KC - 2, KC - 1):
                            slot = 2 * ((b + d // 2) % 2) + d % 2
                            if half == A:
                                pe.wait_ge(lo_ready, 2 * (b + 12) + d + 1)
                            else:
                                pe.wait_ge(m_evac[A], 8 * s + d + 1)
                            last = output_half(bank[d], half, [
                                (w_hi[:, slot, k * P:(k + 1) * P], w_lo[:, slot, k * P:(k + 1) * P],
                                 o_hi[:, k, :], o_lo[:, k, :], k == 0) for k in range(KC)],
                                lambda i: norm_a(s, d, i) if half == B else None)
                            last.then_inc(acc_done[A] if half == A else w_used, 1)
            out_total(NSUB - 1, B)
            out_broadcast(NSUB - 1, B)
            for q in range(2 * TT):
                if q % TT == 0:
                    pe.wait_ge(h_ready[q // TT], 8 * NSUB + 8)
                for c in range(4):
                    last = pe.transpose(bank[TURN[q]][:, c * P:(c + 1) * P],
                                        h[:, 4 * (q % 2) + c, (q // 2) * P:(q // 2 + 1) * P], ident[:, :])
                last.then_inc(out_turned, 1)


_INS = ["x", "norm_pre", "norm_post", "ffn_w_gate", "ffn_w_up", "ffn_w_down", "a_w_in", "a_ln_g", "a_w_s",
        "a_b_s", "a_w_out", "b_w_qkv", "b_w_o"]


def kernel(**inputs):
    import numpy as _np
    import concourse.bacc as _bacc
    from concourse import mybir as _mybir
    from concourse.bass_utils import run_bass_kernel_spmd as _run

    nc = _bacc.Bacc("TRN2", target_bir_lowering=False, num_devices=1)
    arrays, args = {}, []
    for name in _INS:
        a = _np.ascontiguousarray(inputs[name])
        arrays[f"in_{name}_dram"] = a
        args.append(nc.dram_tensor(f"in_{name}_dram", a.shape, _mybir.dt.from_np(a.dtype), kind="ExternalInput").ap())
    args.append(nc.dram_tensor("out_dram", (1, T, DM), F32, kind="ExternalOutput").ap())
    build(nc, *args)
    r = _run(nc, [arrays], core_ids=[0])
    return r.results[0]["out_dram"]
```
